# Optimizing a Trainium2 kernel written in Bass

```python
import math
import jax, jax.numpy as jnp
from jax import lax
import numpy as np

D_MODEL = 1024
BATCH = 1
SEQ = 512
DEPTH = 2

CHUNK = 64
HEAD_DIM = 64
A_HEADS = 8
A_KV_HEADS = 2
A_GROUP = A_HEADS // A_KV_HEADS
A_WINDOW = 128
A_WIN_CHUNKS = A_WINDOW // CHUNK
A_Q = A_HEADS * HEAD_DIM
A_KV = A_KV_HEADS * HEAD_DIM
B_HEADS = 8
B_HEAD_SIZE = 64
B_DIM = B_HEADS * B_HEAD_SIZE
R_DECAY = 64
R_ICLR = 64
R_VRES = 32
R_GATE = 128
B_GN_EPS = 64e-5
B_IN = 3 * B_DIM + R_DECAY + R_ICLR + R_GATE
EVEN_IN = A_Q + 2 * A_KV + B_IN
EVEN_OUT = A_Q + B_DIM
C_HEADS = 8
C_QK_DIM = 64
C_V_DIM = 2 * C_QK_DIM
C_DIM = C_HEADS * C_V_DIM
C_QK_COLS = C_HEADS * 2 * C_QK_DIM
ODD_IN = 2 * C_QK_COLS + C_DIM
SUBLN_EPS = 1e-5
Q_BLOCK = 128
D_FF = 2816
CONV_W = 3
LN_EPS = 1e-5
DEEPNORM_ALPHA = (2.0 * DEPTH) ** 0.25
DEEPNORM_BETA = (8.0 * DEPTH) ** -0.25
N_EVEN = (DEPTH + 1) // 2
N_ODD = DEPTH // 2
NEG_INF = -1e30

kernel_name = 'hybrid_swa_rwkv7_diffattn_encoder'

def alibi_slopes(n_heads):
    return jnp.exp2(-8.0 * jnp.arange(1, n_heads + 1, dtype=jnp.float32) / n_heads)

def layer_norm(x, g, b):
    xf = x.astype(jnp.float32)
    mu = jnp.mean(xf, -1, keepdims=True)
    var = jnp.mean(jnp.square(xf - mu), -1, keepdims=True)
    y = (xf - mu) * lax.rsqrt(var + LN_EPS) * g.astype(jnp.float32) + b.astype(jnp.float32)
    return y.astype(x.dtype)

def token_shift(h):
    return jnp.pad(h[:, :-1], ((0, 0), (1, 0), (0, 0)))

def sliding_window_sink_attention(q, k, v, sinks):
    f32 = jnp.float32
    b, t = q.shape[:2]
    nc = t // CHUNK
    pad = (A_WIN_CHUNKS - 1) * CHUNK
    span = A_WIN_CHUNKS * CHUNK
    qc = q.astype(f32).reshape(b, nc, CHUNK, A_KV_HEADS, A_GROUP, HEAD_DIM)
    kc = jnp.pad(k.astype(f32), ((0, 0), (pad, 0), (0, 0), (0, 0))).reshape(
        b, nc + A_WIN_CHUNKS - 1, CHUNK, A_KV_HEADS, HEAD_DIM)
    vc = jnp.pad(v.astype(f32), ((0, 0), (pad, 0), (0, 0), (0, 0))).reshape(
        b, nc + A_WIN_CHUNKS - 1, CHUNK, A_KV_HEADS, HEAD_DIM)
    kb = jnp.concatenate([kc[:, w:w + nc] for w in range(A_WIN_CHUNKS)], axis=2)
    vb = jnp.concatenate([vc[:, w:w + nc] for w in range(A_WIN_CHUNKS)], axis=2)
    s = jnp.einsum('bcqkgd,bcskd->bckgqs', qc, kb) * (HEAD_DIM ** -0.5)
    dist = jnp.abs(jnp.arange(CHUNK)[:, None] + pad - jnp.arange(span)[None, :]).astype(f32)
    slopes = alibi_slopes(A_HEADS).reshape(A_KV_HEADS, A_GROUP)
    s = s - slopes[:, :, None, None] * dist
    key_pos = jnp.arange(nc)[:, None] * CHUNK - pad + jnp.arange(span)[None, :]
    s = jnp.where((key_pos >= 0)[None, :, None, None, None, :], s, NEG_INF)
    sink = sinks.astype(f32).reshape(A_KV_HEADS, A_GROUP)[None, None, :, :, None, None]
    m = jnp.maximum(jnp.max(s, -1, keepdims=True), sink)
    p = jnp.exp(s - m)
    p = p / (jnp.sum(p, -1, keepdims=True) + jnp.exp(sink - m))
    o = jnp.einsum('bckgqs,bcskd->bcqkgd', p, vb)
    return o.reshape(b, t, A_Q)

def rwkv7_scan(r, w, k, v, a, bb):
    b, t, h, n = r.shape

    def step(S, inp):
        r_t, w_t, k_t, v_t, a_t, b_t = inp
        sa = jnp.einsum('bhij,bhj->bhi', S, a_t)
        S = S * w_t[:, :, None, :] + sa[..., None] * b_t[:, :, None, :] + v_t[..., None] * k_t[:, :, None, :]
        return S, jnp.einsum('bhij,bhj->bhi', S, r_t)

    xs = tuple(jnp.moveaxis(z, 1, 0) for z in (r, w, k, v, a, bb))
    _, y = lax.scan(step, jnp.zeros((b, h, n, n), jnp.float32), xs)
    return jnp.moveaxis(y, 0, 1)

def rwkv7_time_mix(hb, mu, w0, w2, a0, a2, g2, k_k, k_a, r_k, gn_g, gn_b, v_first, vres):
    f32 = jnp.float32
    b, t, _ = hb.shape
    hs = (hb + (token_shift(hb) - hb) * mu).astype(f32)
    cuts = [B_DIM, 2 * B_DIM, 3 * B_DIM, 3 * B_DIM + R_DECAY, 3 * B_DIM + R_DECAY + R_ICLR]
    r, k, v, w_lo, a_lo, g_lo = jnp.split(hs, cuts, axis=-1)
    w = -jax.nn.softplus(-(w0.astype(f32) + jnp.tanh(w_lo) @ w2.astype(f32))) - 0.5
    decay = jnp.exp(-jnp.exp(w))
    a = jax.nn.sigmoid(a0.astype(f32) + a_lo @ a2.astype(f32))
    g = jax.nn.sigmoid(g_lo) @ g2.astype(f32)
    if vres is None:
        v_first = v
    else:
        v0, v1, v2 = vres
        v = v + (v_first - v) * jax.nn.sigmoid(v0.astype(f32) + (v @ v1.astype(f32)) @ v2.astype(f32))

    def heads(z):
        return z.reshape(b, t, B_HEADS, B_HEAD_SIZE)

    kk = heads(k * k_k.astype(f32))
    kk = kk / jnp.maximum(jnp.sqrt(jnp.sum(jnp.square(kk), -1, keepdims=True)), 1e-12)
    k = k * (1.0 + (a - 1.0) * k_a.astype(f32))
    rh, kh, vh = heads(r), heads(k), heads(v)
    y = rwkv7_scan(rh, heads(decay), kh, vh, -kk, kk * heads(a))
    mean = jnp.mean(y, -1, keepdims=True)
    var = jnp.mean(jnp.square(y - mean), -1, keepdims=True)
    y = ((y - mean) * lax.rsqrt(var + B_GN_EPS)).reshape(b, t, B_DIM) * gn_g.astype(f32) + gn_b.astype(f32)
    bonus = jnp.sum(rh * kh * r_k.astype(f32), -1, keepdims=True) * vh
    y = y + bonus.reshape(b, t, B_DIM)
    return y * g, v_first

def differential_attention(h, lam, subln_g, lam_init):
    f32 = jnp.float32
    b, t, _ = h.shape
    q = h[..., :C_QK_COLS].astype(f32).reshape(b, t, C_HEADS, 2, C_QK_DIM) * (C_QK_DIM ** -0.5)
    k = h[..., C_QK_COLS:2 * C_QK_COLS].astype(f32).reshape(b, t, C_HEADS, 2, C_QK_DIM)
    v = h[..., 2 * C_QK_COLS:].astype(f32).reshape(b, t, C_HEADS, C_V_DIM)
    lam = lam.astype(f32)
    lam_full = jnp.exp(jnp.sum(lam[0] * lam[1])) - jnp.exp(jnp.sum(lam[2] * lam[3])) + lam_init
    slopes = alibi_slopes(C_HEADS)[:, None, None, None]
    kpos = jnp.arange(t)
    nqb = t // Q_BLOCK
    q_blocks = jnp.moveaxis(q.reshape(b, nqb, Q_BLOCK, C_HEADS, 2, C_QK_DIM), 1, 0)
    starts = jnp.arange(nqb) * Q_BLOCK

    def one_block(args):
        qb, start = args
        qpos = start + jnp.arange(Q_BLOCK)
        s = jnp.einsum('bqhmd,bshmd->bhmqs', qb, k)
        s = s - slopes * jnp.abs(qpos[:, None] - kpos[None, :]).astype(f32)
        visible = (kpos[None, :] // CHUNK) <= (qpos[:, None] // CHUNK)
        p = jax.nn.softmax(jnp.where(visible, s, NEG_INF), axis=-1)
        attn = p[:, :, 0] - lam_full * p[:, :, 1]
        return jnp.einsum('bhqs,bshd->bqhd', attn, v)

    o = lax.map(one_block, (q_blocks, starts))
    o = jnp.moveaxis(o, 0, 1).reshape(b, t, C_HEADS, C_V_DIM)
    o = o * lax.rsqrt(jnp.mean(jnp.square(o), -1, keepdims=True) + SUBLN_EPS) * subln_g.astype(f32)
    return (o * (1.0 - lam_init)).reshape(b, t, C_DIM)

def conv_gated_mlp(x, w_up, conv_w, conv_b, w_down):
    h = x @ w_up
    h = lax.conv_general_dilated(h, conv_w[:, None, :], window_strides=(1,),
                                 padding=[(CONV_W - 1, 0)],
                                 dimension_numbers=('NWC', 'WIO', 'NWC'),
                                 feature_group_count=2 * D_FF) + conv_b
    u, gate = h[..., :D_FF], h[..., D_FF:]
    return (jax.nn.silu(gate) * u) @ w_down

def setup_inputs(seed: int = 0) -> dict:
    key = jax.random.key(seed)
    keys = jax.random.split(key, 32)
    count = [0]

    def nxt():
        sub = keys[count[0]]
        count[0] += 1
        return sub

    def nrm(shape, scale):
        return scale * jax.random.normal(nxt(), shape, jnp.float32)

    def unif(shape, lo, hi):
        return jax.random.uniform(nxt(), shape, jnp.float32, lo, hi)

    NV = N_EVEN - 1
    return {
        'x': nrm((BATCH, SEQ, D_MODEL), 1.0),
        'ln_g': 1.0 + nrm((DEPTH, 2, D_MODEL), 0.05),
        'ln_b': nrm((DEPTH, 2, D_MODEL), 0.02),
        'ev_w_in': nrm((N_EVEN, D_MODEL, EVEN_IN), D_MODEL ** -0.5),
        'ev_sinks': nrm((N_EVEN, A_HEADS), 1.0),
        'ev_mu': unif((N_EVEN, B_IN), 0.0, 1.0),
        'ev_w0': unif((N_EVEN, B_DIM), -5.0, 0.5),
        'ev_w2': nrm((N_EVEN, R_DECAY, B_DIM), 0.5 * R_DECAY ** -0.5),
        'ev_a0': nrm((N_EVEN, B_DIM), 0.1),
        'ev_a2': nrm((N_EVEN, R_ICLR, B_DIM), 0.5 * R_ICLR ** -0.5),
        'ev_g2': nrm((N_EVEN, R_GATE, B_DIM), R_GATE ** -0.5),
        'ev_k_k': 0.85 + nrm((N_EVEN, B_DIM), 0.05),
        'ev_k_a': 1.0 + nrm((N_EVEN, B_DIM), 0.05),
        'ev_r_k': nrm((N_EVEN, B_HEADS, B_HEAD_SIZE), 0.1),
        'ev_gn_g': 1.0 + nrm((N_EVEN, B_DIM), 0.05),
        'ev_gn_b': nrm((N_EVEN, B_DIM), 0.02),
        'ev_v0': nrm((NV, B_DIM), 0.1),
        'ev_v1': nrm((NV, B_DIM, R_VRES), B_DIM ** -0.5),
        'ev_v2': nrm((NV, R_VRES, B_DIM), 0.5 * R_VRES ** -0.5),
        'ev_w_out': nrm((N_EVEN, EVEN_OUT, D_MODEL), DEEPNORM_BETA * EVEN_OUT ** -0.5),
        'od_w_in': nrm((N_ODD, D_MODEL, ODD_IN), D_MODEL ** -0.5),
        'od_lam': nrm((N_ODD, 4, C_QK_DIM), 0.1),
        'od_subln_g': 1.0 + nrm((N_ODD, C_V_DIM), 0.05),
        'od_w_out': nrm((N_ODD, C_DIM, D_MODEL), DEEPNORM_BETA * C_DIM ** -0.5),
        'ffn_w_up': nrm((DEPTH, D_MODEL, 2 * D_FF), D_MODEL ** -0.5),
        'ffn_conv_w': nrm((DEPTH, CONV_W, 2 * D_FF), CONV_W ** -0.5),
        'ffn_conv_b': nrm((DEPTH, 2 * D_FF), 0.02),
        'ffn_w_down': nrm((DEPTH, D_FF, D_MODEL), DEEPNORM_BETA * D_FF ** -0.5),
    }

def reference(x, ln_g, ln_b, ev_w_in, ev_sinks, ev_mu, ev_w0, ev_w2, ev_a0, ev_a2, ev_g2,
              ev_k_k, ev_k_a, ev_r_k, ev_gn_g, ev_gn_b, ev_v0, ev_v1, ev_v2, ev_w_out,
              od_w_in, od_lam, od_subln_g, od_w_out,
              ffn_w_up, ffn_conv_w, ffn_conv_b, ffn_w_down):
    b, t, _ = x.shape
    v_first = None
    for i in range(DEPTH):
        if i % 2 == 0:
            e = i // 2
            h = x @ ev_w_in[e]
            qa = h[..., :A_Q].reshape(b, t, A_HEADS, HEAD_DIM)
            ka = h[..., A_Q:A_Q + A_KV].reshape(b, t, A_KV_HEADS, HEAD_DIM)
            va = h[..., A_Q + A_KV:A_Q + 2 * A_KV].reshape(b, t, A_KV_HEADS, HEAD_DIM)
            ya = sliding_window_sink_attention(qa, ka, va, ev_sinks[e])
            vres = None if e == 0 else (ev_v0[e - 1], ev_v1[e - 1], ev_v2[e - 1])
            yb, v_first = rwkv7_time_mix(h[..., A_Q + 2 * A_KV:], ev_mu[e], ev_w0[e], ev_w2[e],
                                         ev_a0[e], ev_a2[e], ev_g2[e], ev_k_k[e], ev_k_a[e],
                                         ev_r_k[e], ev_gn_g[e], ev_gn_b[e], v_first, vres)
            y = jnp.concatenate([ya, yb], axis=-1).astype(x.dtype) @ ev_w_out[e]
        else:
            o = i // 2
            lam_init = 0.8 - 0.6 * math.exp(-0.3 * i)
            yc = differential_attention(x @ od_w_in[o], od_lam[o], od_subln_g[o], lam_init)
            y = yc.astype(x.dtype) @ od_w_out[o]
        x = layer_norm(DEEPNORM_ALPHA * x + y, ln_g[i, 0], ln_b[i, 0])
        f = conv_gated_mlp(x, ffn_w_up[i], ffn_conv_w[i], ffn_conv_b[i], ffn_w_down[i])
        x = layer_norm(DEEPNORM_ALPHA * x + f, ln_g[i, 1], ln_b[i, 1])
    return x


_drawn_inputs = setup_inputs


def setup_inputs(seed=0):
    import zlib

    import numpy as np

    out = dict(_drawn_inputs(seed))
    spreads = {}
    factors = {'ev_sinks': 8.0,
     'ev_w2': 8.0,
     'ev_a0': 8.0,
     'ev_k_k': 8.0,
     'ev_k_a': 7.37,
     'ev_gn_g': 7.724,
     'ev_gn_b': 8.0,
     'od_subln_g': 5.847,
     'ffn_conv_b': 6.491}
    for name, (base, spread) in spreads.items():
        noise = np.random.default_rng([zlib.crc32(name.encode()), seed]).standard_normal(out[name].shape)
        drawn = base * np.exp(spread * noise) if base else spread * noise
        out[name] = __import__('jax').numpy.asarray(drawn.astype(out[name].dtype))
    for name, factor in factors.items():
        out[name] = (out[name] * factor).astype(out[name].dtype)
    return out
```

```python
import math
from contextlib import ExitStack

import concourse.bass as bass
from concourse import mybir

ALU = mybir.AluOpType
ACT = mybir.ActivationFunctionType
F32 = mybir.dt.float32
F32R = mybir.dt.float32r
I32 = mybir.dt.int32
U8 = mybir.dt.uint8
AX_X = mybir.AxisListType.X

P = 128
SEQ = 512
NT = SEQ // P
D = 1024
KT = D // P
DEPTH = 2
HD = 64
HEADS = 8
A_Q = HEADS * HD
A_KV = 2 * HD
B_DIM = HEADS * HD
B_TILES = B_DIM // P
B0 = A_Q + 2 * A_KV
EVEN_IN = B0 + 3 * B_DIM + 256
MU_TILES = (EVEN_IN - B0) // P
C_QK = 1024
F = 2816
FT = F // P
ALPHA = (2.0 * DEPTH) ** 0.25
LN_EPS = 1e-5
GN_EPS = 64e-5
SUBLN_EPS = 1e-5
LAM_INIT = 0.8 - 0.6 * math.exp(-0.3)
MASKED = 1e30
DECAY_SCALE = -math.exp(-0.5)
SLOPES = [2.0 ** (-8.0 * (h + 1) / HEADS) for h in range(HEADS)]

SLAB = 2048
COLS = SLAB // KT
ROWS = SLAB // D
W_IN0 = 0
W_OUT0 = W_IN0 + EVEN_IN // COLS
W_UP0 = W_OUT0 + KT // ROWS
W_DN0 = W_UP0 + FT
W_IN1 = W_DN0 + FT // ROWS
W_OUT1 = W_IN1 + 3 * C_QK // COLS
W_UP1 = W_OUT1 + KT // ROWS
W_DN1 = W_UP1 + FT
W_END = W_DN1 + FT // ROWS
IN0_COLS = [B0 + 3 * B_DIM] + [B0 + B_DIM + COLS * s for s in range(2)] + [B0 + COLS * s for s in range(2)] \
    + [B0 + 2 * B_DIM + COLS * s for s in range(2)] + [COLS * s for s in range(2)] + [A_Q]

R_MU, R_A0, R_KK, R_KA, R_RK = 0, 14, 18, 22, 26
N_CHAN = 30
N_CONV = 4 * 2 * FT
CONV_HALF = N_CONV // 2

LEVELS = 6
RW_PE = ["A", "AV", "T0"] + [s + str(k) for k in range(1, LEVELS) for s in ("P", "D", "T")] + ["P6", "D6", "HG", "R", "Y"]
RW_DVE = ["A"] + [f"D{k}" for k in range(1, LEVELS + 1)] + ["R", "Y"]
RW_ACT = ["AV", "T0"] + [s + str(k) for k in range(1, LEVELS) for s in ("P", "T")] + ["P6", "HG", "R"]


def nth(steps, n, step, half):
    return (n * len(steps) + steps.index(step)) * 2 + half + 1


def attention_steps(items):
    steps = []
    for t in range(items + 6):
        now = []
        for kind, lag in (("S", 0), ("C", 1), ("T", 2), ("V", 3)):
            if 0 <= t - lag < items:
                now.append((kind, t - lag))
        for kind, lag in (("G", 7), ("Y", 9)):
            if t >= lag and (t - lag) % 4 == 0:
                now.append((kind, (t - lag) // 4))
        steps.append(now)
    return steps


def transposed_banks(items):
    order = [s for now in attention_steps(items) for s in now if s[0] in "TY"]
    return {s: n for n, s in enumerate(order)}


def staggered(stages):
    return [(stage, t - k) for t in range(NT + len(stages) - 1) for k, stage in enumerate(stages)
            if 0 <= t - k < NT]


def encoder(nc, x, ln_g, ln_b, ev_w_in, ev_sinks, ev_mu, ev_w0, ev_w2, ev_a0, ev_a2, ev_g2, ev_k_k, ev_k_a,
            ev_r_k, ev_gn_g, ev_gn_b, ev_w_out, od_w_in, od_lam, od_subln_g, od_w_out,
            ffn_w_up, ffn_conv_w, ffn_conv_b, ffn_w_down, out):
    with ExitStack() as ctx:
        def sb(name, shape, dt=F32, where=ctx):
            return where.enter_context(nc.sbuf_tensor(name, shape, dt))

        def sem(name):
            return ctx.enter_context(nc.semaphore(name))

        bank_pair = [ctx.enter_context(nc.psum_tensor(f"bank_pair{i}", [P, 2, 512], F32)) for i in range(4)]
        bank = [bank_pair[i // 2][:, i % 2, :] for i in range(8)]

        x_tok = sb("x_tok", [P, NT, D])
        w_raw = sb("w_raw", [P, 2, SLAB])
        w_hi = sb("w_hi", [P, 2, SLAB], F32R)
        w_lo = sb("w_lo", [P, 2, SLAB], F32R)
        ident = sb("ident", [P, P])
        dist_a = sb("dist_a", [P, 2 * P])
        dist_c = sb("dist_c", [P, 4 * P], F32R)
        tri4 = sb("tri4", [P, 4, P], U8)
        merge = sb("merge", [P, LEVELS + 1, P], U8)
        ucum = sb("ucum", [P, P])
        chan = sb("chan", [P, N_CHAN])
        one_minus = sb("one_minus", [P, N_CHAN])
        conv = sb("conv", [P, DEPTH, N_CONV])
        headsel = sb("headsel", [P, B_TILES, HEADS])
        headsel_t = sb("headsel_t", [HEADS, B_TILES, P])
        pairsel = sb("pairsel", [P, 2])
        sinks = sb("sinks", [P, HEADS])
        lam_c = sb("lam_c", [P, 2])
        sub_g = sb("sub_g", [P, 1])
        half_neg = sb("half_neg", [P, HEADS])
        w0_row = sb("w0_row", [1, B_DIM])
        ones_row = sb("ones_row", [1, P])
        small = sb("small", [P, 160])

        with ExitStack() as xs:
            xt_hi = sb("xt_hi", [P, KT, SEQ], F32R, xs)
            xt_lo = sb("xt_lo", [P, KT, SEQ], F32R, xs)
        tok = sb("tok", [P, 4, NT, B_DIM])
        A_TOK, B_TOK, K_TOK, V_TOK = range(4)

        with ExitStack() as m0:
            rw = sb("rw", [P, 4, B_TILES, SEQ], F32, m0)
            RA, RR, RB, RK = range(4)
            yt0 = sb("yt0", [P, KT, SEQ], F32, m0)
            wa = sb("wa", [P, SEQ], F32, m0)
            gate_in = sb("gate_in", [P, SEQ], F32, m0)
            w2a2 = sb("w2a2", [P, B_DIM], F32, m0)
            g2 = sb("g2", [P, B_DIM], F32, m0)
            gn_gb = sb("gn_gb", [P, 2, B_DIM], F32, m0)
            y_tok = sb("y_tok", [P, B_DIM], F32, m0)
            zbd = sb("zbd", [P, B_TILES, P], F32, m0)
            mbd = sb("mbd", [P, B_TILES, P], F32, m0)
            nst = sb("nst", [P, B_TILES, HD], F32, m0)
            with ExitStack() as u:
                prow = sb("prow", [P, 5, P], F32, u)
                lam_in = sb("lam_in", [P, 4, HD], F32, u)
                dist_f = sb("dist_f", [P, 4 * P], F32, u)
                iota_i = sb("iota_i", [P, 4, 512], I32, u)
                mask_t = sb("mask_t", [P, 3, P], I32, u)
            with ExitStack() as u:
                qa = sb("qa", [P, 4, SEQ], F32, u)
                kdup = sb("kdup", [P, 2, SEQ], F32, u)
                va_ch = sb("va_ch", [P, SEQ], F32, u)
                va_tok = sb("va_tok", [P, NT, P], F32, u)
                sa = sb("sa", [P, 3, 2, 2 * P], F32, u)
                pta = sb("pta", [P, 2, 512], F32, u)
                ya = sb("ya", [P, 2, 512], F32, u)
            with ExitStack() as u:
                epos = sb("epos", [P, B_TILES, NT, P + 1], F32, u)
                eneg = sb("eneg", [P, B_TILES, NT, P], F32, u)
                l_tok = sb("l_tok", [P, NT, B_DIM], F32, u)
                sq = sb("sq", [P, B_TILES, SEQ], F32, u)
            with ExitStack() as u:
                mt = sb("mt", [P, 2, 4, 4, P], F32, u)
                tt = sb("tt", [P, 2, 4, P], F32, u)
                tn = sb("tn", [P, 2, 4, P], F32, u)
                pp = sb("pp", [P, 2, 4, P], F32, u)
                av = sb("av", [P, 2, 4, HD], F32, u)
                hg = pp
                r2 = sb("r2", [P, 2, 2, P], F32, u)
            with ExitStack() as u:
                ln_gb0 = sb("ln_gb0", [P, 2, D], F32, u)
                yt_hi0 = sb("yt_hi0", [P, 2, SEQ], F32R, u)
                yt_lo0 = sb("yt_lo0", [P, 2, SEQ], F32R, u)
        with ExitStack() as m1:
            act_t = sb("act_t", [P, FT, SEQ], F32, m1)
            act_hi = sb("act_hi", [P, 2, SEQ], F32R, m1)
            act_lo = sb("act_lo", [P, 2, SEQ], F32R, m1)
            cu = sb("cu", [P, 2, SEQ], F32, m1)
            cg = sb("cg", [P, 2, SEQ], F32, m1)
            ln_gbf = sb("ln_gbf", [P, 2, D], F32, m1)
        with ExitStack() as m2:
            qc = sb("qc", [P, HEADS, SEQ], F32, m2)
            kc = sb("kc", [P, HEADS, SEQ], F32, m2)
            slope_id = sb("slope_id", [P, HEADS, P], F32R, m2)
            vc = sb("vc", [P, NT, D], F32, m2)
            yt1 = sb("yt1", [P, KT, SEQ], F32, m2)
            pc = sb("pc", [P, 2, SEQ], F32, m2)
            ptc = sb("ptc", [P, 2, SEQ], F32, m2)
            yc = sb("yc", [P, 2, 512], F32, m2)
            ysq = sb("ysq", [P, 512], F32, m2)
            ln_gb1 = sb("ln_gb1", [P, 2, D], F32, m2)
            with ExitStack() as u:
                sc = sb("sc", [P, 2, 2, SEQ], F32, u)
            with ExitStack() as u:
                yt_hi1 = sb("yt_hi1", [P, 2, SEQ], F32R, u)
                yt_lo1 = sb("yt_lo1", [P, 2, SEQ], F32R, u)

        rs = y_tok[0:HEADS, :]

        neg_max = small[:, 0:4].rearrange("p (b m) -> p b m", b=2)
        den = small[:, 4:8].rearrange("p (b m) -> p b m", b=2)
        sink_e = small[:, 8:12].rearrange("p (b m) -> p b m", b=2)
        rden = small[:, 12:28].rearrange("p (b h) -> p b h", b=2)
        rms = small[:, 28:32]
        neg_mean = small[:, 32:36]
        shift = small[:, 36:40]
        mv = small[:, 56:64].rearrange("p (n s) -> p n s", n=4)
        rstd = small[:, 64:68]
        gn_m = small[:, 68:76]
        gn_v = small[:, 76:84]
        cn = small[:, 84:100].rearrange("p (j n) -> p j n", j=4)
        zsc = small[:, 100:112].rearrange("p (j n) -> p j n", j=4)
        bonus = small[:, 112:144].rearrange("p (n h) -> p n h", n=4)
        lam_s = small[:, 144:148]
        maxes = small[:, 148:150]
        bn2 = sb("bn2", [P, 2, 2, 6])

        par_rows = sem("par_rows")
        par_gn = sem("par_gn")
        x_in = [sem(f"x_in{n}") for n in range(NT)]
        w_landed = [sem(f"w_landed{i}") for i in range(2)]
        hi_done = sem("hi_done")
        lo_done = sem("lo_done")
        half_slab = sem("half_slab")
        consts_pool = sem("consts_pool")
        consts_dve = sem("consts_dve")
        par_ps = sem("par_ps")
        xt_ps = sem("xt_ps")
        xt_h = sem("xt_h")
        xt_l = sem("xt_l")
        mixed = sem("mixed")
        tile0_free = sem("tile0_free")
        squashed = sem("squashed")
        va_ps = sem("va_ps")
        va_out = sem("va_out")
        a_s = sem("a_s"); a_bias = sem("a_bias"); a_max = sem("a_max"); a_exp = sem("a_exp"); a_den = sem("a_den")
        a_t = sem("a_t"); a_tout = sem("a_tout"); a_v = sem("a_v"); a_y = sem("a_y")
        c_s = sem("c_s"); c_max = sem("c_max"); c_exp = sem("c_exp"); c_p = sem("c_p")
        c_t = sem("c_t"); c_tout = sem("c_tout"); c_v = sem("c_v"); c_yout = sem("c_yout"); c_y = sem("c_y")
        c_slopes = sem("c_slopes"); c_sq = sem("c_sq"); c_rms = sem("c_rms")
        lora = sem("lora")
        lora_out = sem("lora_out")
        cums = sem("cums")
        centred = sem("centred")
        exps = sem("exps")
        kk_sq = sem("kk_sq")
        kk_ss = sem("kk_ss")
        kk_max = sem("kk_max")
        kk_root = sem("kk_root")
        kk_inv = sem("kk_inv")
        kk_bc = sem("kk_bc")
        rk_done = sem("rk_done")
        bon_ps = sem("bon_ps")
        rw_ready = sem("rw_ready")
        tok_ps = sem("tok_ps")
        tok_a = sem("tok_a")
        tok_d = sem("tok_d")
        rw_init = sem("rw_init")
        rw_pe = sem("rw_pe"); rw_dve = sem("rw_dve"); rw_act = sem("rw_act")
        gn_dve = sem("gn_dve"); gn_pool = sem("gn_pool"); gn_ps = sem("gn_ps"); gn_out = sem("gn_out")
        gate_ps = sem("gate_ps"); gated = sem("gated")
        yt_done = sem("yt_done")
        act_split_h = sem("act_split_h")
        act_split = sem("act_split")
        ln_sum = sem("ln_sum")
        ln_rstd = sem("ln_rstd")
        ln_norm = sem("ln_norm")
        ln_mul = sem("ln_mul")
        acc_tile = sem("acc_tile")
        ln_x = sem("ln_x")
        gb_in = [sem(f"gb_in{i}") for i in range(4)]
        conv_a = sem("conv_a")
        conv_d = sem("conv_d")
        silu_a = sem("silu_a")
        tile1_a = sem("tile1_a"); tile1_d = sem("tile1_d")
        dve_at = sem("dve_at")
        act_at = sem("act_at")
        pool_at = sem("pool_at")
        stored = sem("stored")

        MIX_COUNT = 14
        A_ITEMS, C_ITEMS = 16, 32
        A_BANKS, C_BANKS = transposed_banks(A_ITEMS), transposed_banks(C_ITEMS)

        def slot(n):
            return n % 2

        def w_cols(t, n):
            return t[:, slot(n), :].rearrange("p (k c) -> p k c", k=KT)

        def w_pair(t, n):
            return t[:, slot(n), :].rearrange("p (u k c) -> p u k c", u=2, k=KT)

        def w_rows(t, n):
            return t[:, slot(n), :].rearrange("p (r c) -> p r c", r=ROWS)

        block = ctx.enter_context(nc.Block())

        @block.sync
        def _(sp):
            def load(n, first, dst, src, at=0):
                sp.dma_start(dst, src).then_inc(w_landed[slot(first)], 16)

            def raw_free(n, late=True):
                if late:
                    sp.wait_ge(lo_done, n - 1)

            in0 = ev_w_in[0].rearrange("(k p) c -> p k c", p=P)
            for s, c0 in enumerate(IN0_COLS):
                raw_free(s, s >= 2)
                for h in range(2):
                    sp.dma_start(w_cols(w_raw, s)[:, 4 * h:4 * h + 4, :], in0[:, 4 * h:4 * h + 4, c0:c0 + COLS]) \
                        .then_inc(w_landed[slot(s)], 16)

            def rows_slab(base, w, n0, i, s):
                n = base + n0 + s
                sp.wait_ge(lo_done, n - 1 + 2 * i)
                for r in range(ROWS):
                    sp.dma_start(w_rows(w_raw, n)[:, r, :], w[bass.ds((2 * i + n0 + s) * ROWS * P + r * P, P), :]) \
                        .then_inc(w_landed[slot(n)], 16)

            def out_rows(base, w):
                for s in range(KT // ROWS):
                    rows_slab(base, w, s, 0, 0)

            def up(base, w):
                wv = w.rearrange("(k p) c -> p k c", p=P)
                with sp.Fori(0, FT // 2) as i:
                    for s in range(2):
                        sp.wait_ge(lo_done, base + s - 1 + 2 * i)
                        for u in range(2):
                            sp.dma_start(w_pair(w_raw, base + s)[:, u], wv[:, :, bass.ds(i * 2 * P + s * P + u * F, P)]) \
                                .then_inc(w_landed[slot(base + s)], 16)

            def down(base, w):
                with sp.Fori(0, (FT // ROWS) // 2) as i:
                    for s in range(2):
                        rows_slab(base, w, 0, i, s)
                rows_slab(base, w, FT // ROWS - 1, 0, 0)

            out_rows(W_OUT0, ev_w_out[0])
            up(W_UP0, ffn_w_up[0])
            down(W_DN0, ffn_w_down[0])
            in1 = od_w_in[0].rearrange("(k p) c -> p k c", p=P)
            with sp.Fori(0, (W_OUT1 - W_IN1) // 2) as i:
                for s in range(2):
                    sp.wait_ge(lo_done, W_IN1 + s - 1 + 2 * i)
                    for h in range(2):
                        sp.dma_start(w_cols(w_raw, W_IN1 + s)[:, 4 * h:4 * h + 4, :],
                                     in1[:, 4 * h:4 * h + 4, bass.ds(i * 2 * COLS + s * COLS, COLS)]) \
                            .then_inc(w_landed[slot(W_IN1 + s)], 16)
            out_rows(W_OUT1, od_w_out[0])
            up(W_UP1, ffn_w_up[1])
            down(W_DN1, ffn_w_down[1])
            for n in range(NT):
                sp.wait_ge(ln_x, 3 * NT + n + 1)
                sp.dma_start(out[0, n * P:(n + 1) * P, :], x_tok[:, n, :]).then_inc(stored, 16)
            sp.wait_ge(stored, 16 * NT)

        @block.gpsimd
        def _(pool):
            at = [0]

            def link(ins):
                at[0] += 1
                ins.then_inc(pool_at, 1)
                pool.wait_ge(pool_at, at[0])

            def split(n, i=0):
                pool.wait_ge(hi_done, n + 1 + 2 * i)
                pool.tensor_tensor(w_lo[:, slot(n), :], w_raw[:, slot(n), :], w_hi[:, slot(n), :].bitcast(F32),
                                   ALU.subtract).then_inc(lo_done, 1)

            def norm_round(l):
                gb = (ln_gb0, ln_gbf, ln_gb1, ln_gbf)[l]
                for stage, n in staggered(("scale", "add")):
                    if stage == "scale":
                        pool.wait_ge(ln_sum, 2 * (l * NT + n + 1))
                        link(pool.tensor_tensor(rstd[:, n:n + 1], mv[:, n, 1:2], half_neg[:, 0:1], ALU.pow))
                        pool.tensor_tensor(shift[:, n:n + 1], neg_mean[:, n:n + 1], rstd[:, n:n + 1], ALU.mult) \
                            .then_inc(ln_rstd, 1)
                    else:
                        if n == 0:
                            pool.wait_ge(gb_in[l], 32)
                        pool.wait_ge(ln_mul, l * NT + n + 1)
                        pool.tensor_tensor(x_tok[:, n, :], x_tok[:, n, :], gb[:, 1, :], ALU.add).then_inc(ln_x, 1)

            pool.memset(ident[:], 0.0).then_inc(pool_at, 1)
            pool.memset(headsel[:], 1.0).then_inc(pool_at, 1)
            pool.memset(headsel_t[:], 1.0).then_inc(pool_at, 1)
            pool.memset(pairsel[:], 0.0).then_inc(pool_at, 1)
            at[0] = 4
            pool.wait_ge(pool_at, 4)
            pool.affine_select(out=ident[:], in_=ident[:], compare_op=ALU.not_equal, fill=1.0, base=0,
                               pattern=[[-1, P]], channel_multiplier=1).then_inc(consts_pool, 1)
            pool.iota(iota_i[:, 0, :], [[-1, 4 * P]], base=3 * P, channel_multiplier=1).then_inc(consts_pool, 1)
            pool.iota(iota_i[:, 1, 0:P], [[1, P]], base=0, channel_multiplier=-1).then_inc(consts_pool, 1)
            pool.iota(iota_i[:, 2, 0:P], [[1, P]], base=0, channel_multiplier=0).then_inc(consts_pool, 1)
            pool.iota(iota_i[:, 3, 0:P], [[0, P]], base=0, channel_multiplier=1).then_inc(consts_pool, 1)
            link(pool.affine_select(out=headsel[:], in_=headsel[:], compare_op=ALU.is_ge, fill=0.0, base=0,
                                    pattern=[[P, B_TILES], [-HD, HEADS]], channel_multiplier=1))
            pool.affine_select(out=headsel[:], in_=headsel[:], compare_op=ALU.is_ge, fill=0.0, base=HD - 1,
                               pattern=[[-P, B_TILES], [HD, HEADS]], channel_multiplier=-1).then_inc(consts_pool, 1)
            link(pool.affine_select(out=headsel_t[:], in_=headsel_t[:], compare_op=ALU.is_ge, fill=0.0, base=0,
                                    pattern=[[P, B_TILES], [1, P]], channel_multiplier=-HD))
            pool.affine_select(out=headsel_t[:], in_=headsel_t[:], compare_op=ALU.is_ge, fill=0.0, base=HD - 1,
                               pattern=[[-P, B_TILES], [-1, P]], channel_multiplier=HD).then_inc(consts_pool, 1)
            pool.memset(pairsel[0:HD, 0:1], 1.0).then_inc(consts_pool, 1)
            pool.memset(pairsel[HD:P, 1:2], 1.0).then_inc(consts_pool, 1)
            pool.wait_ge(consts_pool, 9)
            pool.memset(half_neg[:], -0.5).then_inc(consts_pool, 1)
            pool.memset(ones_row[:], 1.0).then_inc(consts_pool, 1)
            pool.memset(zbd[:], 0.0).then_inc(consts_pool, 1)
            pool.memset(mbd[:], 0.0).then_inc(consts_pool, 1)

            for n in range(W_UP0):
                split(n)
                if n == W_OUT0 + 1:
                    pool.wait_ge(rw_ready, B_TILES)
                    pool.wait_ge(bon_ps, 1)
                    for h in range(2):
                        pool.memset(mt[:, h], 0.0).then_inc(rw_init, 1)
                    for c in range(NT):
                        pool.wait_ge(gn_dve, 4 * c + 1)
                        pool.tensor_tensor(tok[:, A_TOK, c, :], y_tok[:], y_tok[:], ALU.mult).then_inc(gn_pool, 1)
                        pool.wait_ge(gn_dve, 4 * c + 2)
                        pool.tensor_tensor(gn_v, gn_v, half_neg[:], ALU.pow).then_inc(gn_pool, 1)
                        pool.wait_ge(gn_dve, 4 * c + 3)
                        if c == 0:
                            pool.wait_ge(par_gn, 32)
                        link(pool.tensor_tensor(y_tok[:], y_tok[:], gn_gb[:, 0, :], ALU.mult))
                        link(pool.tensor_tensor(y_tok[:], y_tok[:], gn_gb[:, 1, :], ALU.add))
                        pool.wait_ge(gn_dve, 4 * c + 4)
                        pool.tensor_tensor(y_tok[:], y_tok[:], tok[:, V_TOK, c, :], ALU.add).then_inc(gn_pool, 1)
            split(W_UP0)
            norm_round(0)
            split(W_UP0 + 1)
            with pool.Fori(0, (W_IN1 + 1 - W_UP0 - 2) // 2) as i:
                split(W_UP0 + 2, i)
                split(W_UP0 + 3, i)
            norm_round(1)
            split(W_IN1 + 1)
            with pool.Fori(0, (W_OUT1 - W_IN1 - 2) // 2) as i:
                split(W_IN1 + 2, i)
                split(W_IN1 + 3, i)
            split(W_OUT1)
            split(W_OUT1 + 1)
            for g in range(C_ITEMS // 4):
                pool.wait_ge(c_sq, 3 * g + 3)
                pool.tensor_tensor(rms, rms, half_neg[:, 0:4], ALU.pow).then_inc(c_rms, 1)
            for n in range(W_OUT1 + 2, W_UP1 + 1):
                split(n)
            norm_round(2)
            split(W_UP1 + 1)
            with pool.Fori(0, (W_END - W_UP1 - 3) // 2) as i:
                split(W_UP1 + 2, i)
                split(W_UP1 + 3, i)
            split(W_END - 1)
            norm_round(3)

        @block.scalar
        def _(act):
            at = [0]

            def link(ins):
                at[0] += 1
                ins.then_inc(act_at, 1)
                act.wait_ge(act_at, at[0])

            def split(n, i=0, first=False):
                act.wait_ge(w_landed[slot(n)], 32 * (n // 2 + 1) + 32 * i)
                if not first:
                    act.wait_ge(half_slab, 2 * (n - 1) + 4 * i)
                act.activation(w_hi[:, slot(n), :], w_raw[:, slot(n), :], ACT.Copy).then_inc(hi_done, 1)

            def x_high(r, n):
                if True:
                    for h in range(2):
                        act.wait_ge(xt_ps, 8 * r + 2 * n + h + 1)
                        act.activation(xt_hi[:, 4 * h:4 * h + 4, n * P:(n + 1) * P],
                                       bank[2 * n + h].rearrange("p (k t) -> p k t", k=4), ACT.Copy).then_inc(xt_h, 1)

            def norm(l):
                for stage, n in staggered(("normalise", "transposed", "high")):
                    if stage == "normalise":
                        act.wait_ge(ln_rstd, l * NT + n + 1)
                        act.activation(x_tok[:, n, :], x_tok[:, n, :], ACT.Identity, bias=shift[:, n:n + 1],
                                       scale=rstd[:, n:n + 1]).then_inc(ln_norm, 1)
                    elif stage == "high" and l < 3:
                        x_high(l + 1, n)

            def load_gb(l, gb):
                act.dma_start(gb[:, 0, :], ln_g[l // 2, l % 2, :].partition_broadcast(P)).then_inc(gb_in[l], 16)
                act.dma_start(gb[:, 1, :], ln_b[l // 2, l % 2, :].partition_broadcast(P)).then_inc(gb_in[l], 16)

            def attention(items, banks, tiles, s_max, s_exp, s_t, s_tout, scores, probs, negs, dens, pt, sink, target, scale):
                for now in attention_steps(items):
                    for kind, i in now:
                        if kind == "S":
                            act.wait_ge(s_max, i + 1)
                            width = tiles(i)
                            for m in range(2):
                                ins = act.activation(probs(i, m, width), scores(i, m, width), ACT.Exp,
                                                     bias=negs(i)[:, m:m + 1], accum_out=dens(i)[:, m:m + 1])
                                if m == 1 and not sink:
                                    ins.then_inc(s_exp, 1)
                            if sink:
                                act.activation(sink_e[:, i % 2, :], sink_e[:, i % 2, :], ACT.Exp).then_inc(s_exp, 1)
                        elif kind in "TY":
                            use = banks[(kind, i)]
                            act.wait_ge(s_t, use + 1)
                            if kind == "T":
                                nb = tiles(i) // P * (2 if sink else 1)
                                act.activation(pt[:, i % 2, 0:nb * P], bank[4 + use % 2][:, 0:nb * P], ACT.Copy) \
                                    .then_inc(s_tout, 1)
                            else:
                                src = bank[4 + use % 2][:].rearrange("p (c t) -> p c t", c=4)
                                if scale is None:
                                    act.activation(target(i), src, ACT.Copy).then_inc(s_tout, 1)
                                else:
                                    act.activation(target(i), src, ACT.Copy, scale=scale).then_inc(s_tout, 1)

            act.nop().then_inc(tile1_a, 4)
            for n in range(NT):
                act.dma_start(x_tok[:, n, :], x[0, n * P:(n + 1) * P, :]).then_inc(x_in[n], 16)
            rows = [(0, R_MU, ev_mu[0].rearrange("(t p) -> t p", p=P)),
                    (0, R_A0, ev_a0[0].rearrange("(t p) -> t p", p=P)),
                    (0, R_KK, ev_k_k[0].rearrange("(t p) -> t p", p=P)),
                    (0, R_KA, ev_k_a[0].rearrange("(t p) -> t p", p=P)),
                    (0, R_RK, ev_r_k[0].rearrange("(t e) d -> t (e d)", e=2)),
                    (0, N_CHAN, od_subln_g)]
            for k, r0, src in rows:
                act.dma_start(prow[r0:r0 + src.shape[0], k, :], src).then_inc(par_rows, 16)
            n_rows = len(rows)
            for l in range(DEPTH):
                src = ffn_conv_w[l].rearrange("w (t p) -> (w t) p", p=P)
                act.dma_start(prow[0:CONV_HALF, 1 + 2 * l, :], src[0:CONV_HALF]).then_inc(par_rows, 16)
                act.dma_start(prow[0:3 * 2 * FT - CONV_HALF, 2 + 2 * l, :], src[CONV_HALF:3 * 2 * FT]).then_inc(par_rows, 16)
                act.dma_start(prow[3 * 2 * FT - CONV_HALF:CONV_HALF, 2 + 2 * l, :],
                              ffn_conv_b[l].rearrange("(t p) -> t p", p=P)).then_inc(par_rows, 16)
                n_rows += 3
            act.dma_start(w2a2[0:HD, :], ev_w2[0]).then_inc(par_rows, 16)
            act.dma_start(w2a2[HD:P, :], ev_a2[0]).then_inc(par_rows, 16)
            act.dma_start(g2[:], ev_g2[0]).then_inc(par_rows, 16)
            act.dma_start(w0_row[:], ev_w0).then_inc(par_rows, 16)
            act.dma_start(sinks[:], ev_sinks[0].partition_broadcast(P)).then_inc(par_rows, 16)
            act.dma_start(lam_in[:], od_lam[0].partition_broadcast(P)).then_inc(par_rows, 16)
            n_rows += 6
            assert n_rows == N_PARAM_DMAS
            act.dma_start(gn_gb[:, 0, :], ev_gn_g[0].partition_broadcast(P)).then_inc(par_gn, 16)
            act.dma_start(gn_gb[:, 1, :], ev_gn_b[0].partition_broadcast(P)).then_inc(par_gn, 16)

            for n in range(NT):
                x_high(0, n)
                if n == 1:
                    split(0, first=True)
            split(1, first=True)
            act.wait_ge(consts_dve, 2)
            act.activation(lam_s[:, 2:4], lam_s[:, 0:2], ACT.Exp).then_inc(squashed, 1)

            def mix_target(t):
                if t == 0:
                    return wa[:]
                if t == 1:
                    return gate_in[:]
                j, which = (t - 2) % 4, (t - 2) // 4
                return (rw[:, RK, j, :], rw[:, RR, j, :], yt0[:, 4 + j, :])[which]

            def mix_row(t):
                return 12 + t if t < 2 else (4 + t - 2, t - 6, 8 + t - 10)[(t - 2) // 4]

            act.wait_ge(consts_dve, 3)
            for s in range(W_OUT0):
                for c in range(2):
                    t = 2 * s + c
                    if t < MIX_COUNT:
                        act.wait_ge(half_slab, t + 1)
                        r = mix_row(t)
                        act.activation(mix_target(t), bank[t % 4][:], ACT.Copy, scale=one_minus[:, r:r + 1]).then_inc(mixed, 1)
                split(s + 2)
                if s == 1:
                    act.wait_ge(tile0_free, 4 + 2)
                    act.activation(wa[0:HD, :], wa[0:HD, :], ACT.Tanh).then_inc(squashed, 1)
                    act.activation(gate_in[:], gate_in[:], ACT.Sigmoid).then_inc(squashed, 1)

            attention(A_ITEMS, A_BANKS, lambda i: P if i < 4 else 2 * P, a_max, a_exp, a_t, a_tout,
                      lambda i, m, w: sa[:, i % 3, m, 2 * P - w:2 * P],
                      lambda i, m, w: sa[:, i % 3, m, 2 * P - w:2 * P], lambda i: neg_max[:, i % 2, :],
                      lambda i: den[:, i % 2, :], pta, True, lambda g: yt0[:, 0:4, g * P:(g + 1) * P], None)

            for n in range(NT):
                act.wait_ge(lora, n + 1)
                act.activation(l_tok[:, n, :], bank[n][:], ACT.Sigmoid).then_inc(lora_out, 1)
            for j in range(B_TILES):
                act.wait_ge(lora, NT + j + 1)
                act.activation(rw[:, RB, j, :], bank[4 + j][:], ACT.Sigmoid, bias=chan[:, R_A0 + j:R_A0 + j + 1]) \
                    .then_inc(lora_out, 1)
            act.wait_ge(kk_max, 1)
            act.activation(rs, rs, ACT.Sqrt).then_inc(kk_root, 1)
            for j in range(B_TILES):
                act.wait_ge(centred, 3 * j + 3)
                act.activation(eneg[:, j], epos[:, j, :, 1:P + 1], ACT.Exp, scale=-1.0).then_inc(act_at, 1)
                at[0] += 1
                act.wait_ge(act_at, at[0])
                act.activation(epos[:, j], epos[:, j], ACT.Exp).then_inc(exps, 1)
            act.wait_ge(centred, 3 * B_TILES + 1)
            act.activation(zsc, zsc, ACT.Exp).then_inc(exps, 1)
            for g in range(16):
                if g % 2 == 0:
                    act.wait_ge(tok_ps, g + 1)
                    act.activation(tok[:, g // 4, g % 4, :], bank[g % 8][:], ACT.Copy).then_inc(tok_a, 1)

            def rw_step(n, step, h):
                act.wait_ge(rw_pe, nth(RW_PE, n, step, h))
                if step == "AV":
                    dst, src = av[:, h], bank[4 * h + 3][:, 0:4 * HD].rearrange("p (a c) -> p a c", a=4)
                elif step[0] == "T":
                    dst, src = tn[:, h], bank[4 * h][:].rearrange("p (a c) -> p a c", a=4)
                elif step[0] == "P":
                    dst, src = pp[:, h], bank[4 * h + 1][:].rearrange("p (a c) -> p a c", a=4)
                elif step == "HG":
                    dst, src = hg[:, h], bank[4 * h][:].rearrange("p (a c) -> p a c", a=4)
                else:
                    dst = nst[:, 2 * h:2 * h + 2, :]
                    src = bank[4 * h + 3][:, 2 * P:3 * P].rearrange("p (a c) -> p a c", a=2)
                act.activation(dst, src, ACT.Copy).then_inc(rw_act, 1)

            def gn_transposed(n):
                act.wait_ge(gn_ps, n + 1)
                act.activation(yt0[:, 4:8, n * P:(n + 1) * P], bank[3][:].rearrange("p (c t) -> p c t", c=4), ACT.Copy) \
                    .then_inc(gn_out, 1)

            for n in range(NT):
                for step in RW_ACT:
                    for h in range(2):
                        rw_step(n, step, h)
                    if step == "P6" and n > 0:
                        gn_transposed(n - 1)
            gn_transposed(NT - 1)
            load_gb(0, ln_gb0)

            def out_projection(base):
                for s in range(KT // ROWS):
                    split(base + s + 2) if s < KT // ROWS - 1 else None

            out_projection(W_OUT0)
            norm(0)
            split(W_UP0 + 1)
            load_gb(1, ln_gbf)

            def mlp(base, layer, last):
                cw = conv[:, layer, :].rearrange("p (w u f) -> p w u f", w=4, u=2)
                with act.Fori(0, FT // 2) as i:
                    for s in range(2):
                        for u, buf in enumerate((cu, cg)):
                            act.wait_ge(half_slab, 2 * (base + s) + u + 1 + 4 * i)
                            act.wait_ge(conv_d, layer * 5 * FT + 5 * s + 5 + 10 * i)
                            act.activation(buf[:, s, :], bank[2 * s + u][:], ACT.Identity,
                                           bias=cw[:, 3, u, bass.ds(2 * i + s, 1)],
                                           scale=cw[:, 2, u, bass.ds(2 * i + s, 1)]).then_inc(conv_a, 1)
                        split(base + 2 + s, i)
                        act.wait_ge(conv_d, 10 + layer * 5 * FT + 5 * s + 4 + 10 * i)
                        act.activation(cg[:, s, :], cg[:, s, :], ACT.Silu).then_inc(silu_a, 1)
                n_down = FT // ROWS - (2 if last else 0)
                with act.Fori(0, n_down // 2) as i:
                    split(base + FT + 2, i)
                    split(base + FT + 3, i)
                if n_down % 2 and last:
                    split(base + FT + 2 + n_down - 1)

            mlp(W_UP0, 0, False)
            norm(1)
            split(W_IN1 + 1)
            load_gb(2, ln_gb1)

            with act.Fori(0, 2) as i:
                for s in range(2):
                    split(W_IN1 + 2 + s, i)
            with act.Fori(0, 2) as i:
                for s in range(2):
                    for c in range(2):
                        act.wait_ge(half_slab, 2 * W_IN1 + 8 + 2 * s + c + 1 + 4 * i)
                        act.activation(kc[:, bass.ds(4 * i + 2 * s + c, 1), :].rearrange("p o t -> p (o t)"),
                                       bank[2 * s + c][:], ACT.Copy).then_inc(tile1_a, 1)
                    split(W_IN1 + 6 + s, i)
            with act.Fori(0, 2) as i:
                for s in range(2):
                    split(W_IN1 + 10 + s, i)

            attention(C_ITEMS, C_BANKS, lambda i: P * (i // 8 + 1), c_max, c_exp, c_t, c_tout,
                      lambda i, m, w: bank[(i % 2) * 2 + m][:, 0:w], lambda i, m, w: sc[:, i % 2, m, 0:w],
                      lambda i: neg_max[:, i % 2, :],
                      lambda i: den[:, i % 2, :], ptc, False,
                      lambda g: yt1[:, 4 * (g % 2):4 * (g % 2) + 4, (g // 2) * P:(g // 2 + 1) * P], sub_g[:, 0:1])
            out_projection(W_OUT1)
            norm(2)
            split(W_UP1 + 1)
            load_gb(3, ln_gbf)
            mlp(W_UP1, 1, True)
            norm(3)

        @block.tensor
        def _(pe):
            def three(psum, hi, lo, rhi, rlo, start, stop):
                pe.matmul(psum, hi, rhi, start=start, stop=False)
                pe.matmul(psum, hi, rlo, start=False, stop=False)
                return pe.matmul(psum, lo, rhi, start=False, stop=stop)

            def x_transposed(r):
                for n in range(NT):
                    if r == 0:
                        pe.wait_ge(x_in[n], 16)
                    else:
                        pe.wait_ge(ln_x, (r - 1) * NT + n + 1)
                    for h in range(2):
                        for k in range(4):
                            c = 4 * h + k
                            ins = pe.transpose(bank[2 * n + h][:, k * P:(k + 1) * P], x_tok[:, n, c * P:(c + 1) * P], ident[:])
                        ins.then_inc(xt_ps, 1)

            def first_slab(n, r, width, columns):
                hi, lo = columns(w_hi, n), columns(w_lo, n)
                pe.wait_ge(lo_done, n + 1)
                for t in range(2):
                    pe.wait_ge(xt_l, 8 * r + 4 * (t + 1))
                    tokens = slice(2 * t * P, 2 * (t + 1) * P)
                    for c in range(2):
                        if t == 0:
                            width(c)
                        for k in range(KT):
                            cols = (hi[:, c, k, :], lo[:, c, k, :]) if columns is w_pair else \
                                (hi[:, k, c * P:(c + 1) * P], lo[:, k, c * P:(c + 1) * P])
                            ins = three(bank[c][:, tokens], *cols, xt_hi[:, k, tokens], xt_lo[:, k, tokens],
                                        k == 0, k == KT - 1)
                        if t == 1:
                            ins.then_inc(half_slab, 1)

            def column_tile(n, c, psum):
                hi, lo = w_cols(w_hi, n), w_cols(w_lo, n)
                for k in range(KT):
                    ins = three(psum, hi[:, k, c * P:(c + 1) * P], lo[:, k, c * P:(c + 1) * P], xt_hi[:, k, :],
                                xt_lo[:, k, :], k == 0, k == KT - 1)
                ins.then_inc(half_slab, 1)

            def row_tiles(n, i, hi, lo, first, last, f0, used=True):
                pe.wait_ge(lo_done, n + 1 + 2 * i)
                order = [(r, t) for t in range(NT) for r in range(ROWS)] if last else \
                    [(r, t) for r in range(ROWS) for t in range(NT)]
                for r, t in order:
                    if t == 0:
                        pe.wait_ge(act_split, f0 + r + 1 + 2 * ROWS * i)
                    wh, wl = w_rows(w_hi, n)[:, r, :], w_rows(w_lo, n)[:, r, :]
                    ah, al = hi[:, r, t * P:(t + 1) * P], lo[:, r, t * P:(t + 1) * P]
                    for q, (a, w) in enumerate(((ah, wh), (ah, wl), (al, wh))):
                        for h in range(2):
                            ins = pe.matmul(bank[2 * t + h][:], a, w[:, h * 512:(h + 1) * 512],
                                            start=first and r == 0 and q == 0, stop=last and r == ROWS - 1 and q == 2)
                    if t == NT - 1:
                        ins.then_inc(half_slab, 1)
                    elif last and r == ROWS - 1:
                        ins.then_inc(acc_tile, 1)

            def out_projection(base, hi, lo, f0):
                for s in range(KT // ROWS):
                    row_tiles(base + s, 0, hi, lo, s == 0, s == KT // ROWS - 1, f0 + ROWS * s)

            def attention(items, banks, tiles, s_s, s_read, per, bias, s_p, s_t, s_tout, s_v, s_yout, s_y, score, probs, value, y):
                for now in attention_steps(items):
                    for kind, i in now:
                        nb = tiles(i) if kind in "STV" else 4
                        if kind == "S":
                            if i >= 2:
                                pe.wait_ge(s_read, per * (i - 1))
                            for m in range(2):
                                q, k = score(i, m)
                                ins = pe.matmul(bank[(i % 2) * 2 + m][:, 0:nb * P], q, k, start=True, stop=bias is None)
                            if bias is not None:
                                for m in range(2):
                                    ins = pe.matmul(bank[(i % 2) * 2 + m][:, 0:nb * P], *bias(i), start=False, stop=True)
                            ins.then_inc(s_s, 1)
                        elif kind in "TY":
                            use = banks[(kind, i)]
                            pe.wait_ge(s_p if kind == "T" else s_y, i + 1)
                            if use >= 2:
                                pe.wait_ge(s_tout, use - 1)
                            blocks = probs(i) if kind == "T" else [y(i)[:, b * P:(b + 1) * P] for b in range(4)]
                            for b, blk in enumerate(blocks):
                                ins = pe.transpose(bank[4 + use % 2][:, b * P:(b + 1) * P], blk, ident[:])
                            ins.then_inc(s_t, 1)
                        elif kind == "V":
                            pe.wait_ge(s_tout, banks[("T", i)] + 1)
                            if i % 4 == 0 and i >= 8:
                                pe.wait_ge(s_yout, i // 4 - 1)
                            for dst, terms in value(i):
                                for b, (p, v) in enumerate(terms):
                                    ins = pe.matmul(bank[6 + i // 4 % 2][:, dst], p, v, start=b == 0, stop=b == len(terms) - 1)
                            ins.then_inc(s_v, 1)

            pe.wait_ge(consts_pool, 1)
            x_transposed(0)
            first_slab(0, 0, lambda c: pe.wait_ge(tile0_free, c + 1), w_cols)
            pe.wait_ge(par_rows, 16 * N_PARAM_DMAS)
            pe.transpose(bank[6][:, 0:N_CHAN + 1], prow[0:N_CHAN + 1, 0, :], ident[0:N_CHAN + 1, 0:N_CHAN + 1])
            for q in range(4):
                ins = pe.transpose(bank[7][:, q * CONV_HALF:(q + 1) * CONV_HALF], prow[0:CONV_HALF, 1 + q, :],
                                   ident[0:CONV_HALF, 0:CONV_HALF])
            ins.then_inc(par_ps, 1)

            pe.wait_ge(lo_done, 2)
            for c in range(2):
                pe.wait_ge(tile0_free, 3 + c)
                column_tile(1, c, bank[2 + c])
            with pe.Fori(1, W_OUT0 // 2) as i:
                for s in range(2):
                    pe.wait_ge(lo_done, s + 1 + 2 * i)
                    for c in range(2):
                        t = 2 * s + c
                        pe.wait_ge(tile0_free, t + 1 + 4 * i)
                        column_tile(s, c, bank[t][:])
            pe.wait_ge(tile0_free, 24)

            for n in range(NT):
                ins = pe.transpose(bank[0][:, n * P:(n + 1) * P], va_ch[:, n * P:(n + 1) * P], ident[:])
            ins.then_inc(va_ps, 1)
            pe.wait_ge(va_out, 1)

            def a_score(i, m):
                n, j = i // 4, i % 4
                lo = max(n - 1, 0) * P
                return (qa[m * HD:(m + 1) * HD, j, n * P:(n + 1) * P],
                        kdup[m * HD:(m + 1) * HD, j // 2, lo:(n + 1) * P])

            def a_probs(i):
                nb = 1 if i < 4 else 2
                return [sa[:, i % 3, m, (2 - nb + b) * P:(3 - nb + b) * P] for m in range(2) for b in range(nb)]

            def a_value(i):
                n, j = i // 4, i % 4
                nb = 1 if n == 0 else 2
                return [(slice((2 * j + m) * HD, (2 * j + m + 1) * HD),
                         [(pta[:, i % 2, (m * nb + b) * P:(m * nb + b + 1) * P],
                           va_tok[:, n + 1 - nb + b, (j // 2) * HD:(j // 2 + 1) * HD]) for b in range(nb)])
                        for m in range(2)]

            attention(A_ITEMS, A_BANKS, lambda i: 1 if i < 4 else 2, a_s, a_bias, 2, None, a_exp, a_t, a_tout, a_v, a_y, a_y,
                      a_score, a_probs, a_value, lambda g: ya[:, g % 2, :])
            pe.wait_ge(a_tout, len(A_BANKS))

            pe.wait_ge(squashed, 3)
            pe.wait_ge(consts_pool, 13)
            pe.wait_ge(a_bias, 2 * A_ITEMS)
            for n in range(NT):
                pe.matmul(bank[n][:], ones_row[:], w0_row[:], start=True, stop=False)
                pe.matmul(bank[n][:], wa[0:HD, n * P:(n + 1) * P], w2a2[0:HD, :], start=False, stop=True).then_inc(lora, 1)
            for j in range(B_TILES):
                pe.matmul(bank[4 + j][:], w2a2[HD:P, j * P:(j + 1) * P], wa[HD:P, :], start=True, stop=True).then_inc(lora, 1)
            pe.wait_ge(lora_out, NT)
            for j in range(B_TILES):
                for n in range(NT):
                    ins = pe.matmul(bank[j][:, n * P:(n + 1) * P], l_tok[:, n, j * P:(j + 1) * P], ucum[:],
                                    start=True, stop=True)
                ins.then_inc(cums, 1)
            pe.wait_ge(lora_out, NT + B_TILES)
            pe.wait_ge(kk_sq, B_TILES)
            for j in range(B_TILES):
                ins = pe.matmul(bank[4][0:HEADS, :], headsel[:, j, :], sq[:, j, :], start=j == 0, stop=j == B_TILES - 1)
            ins.then_inc(kk_ss, 1)
            pe.wait_ge(kk_inv, 1)
            for j in range(B_TILES):
                pe.matmul(bank[4 + j][:], headsel_t[:, j, :], rs, start=True, stop=True).then_inc(kk_bc, 1)
            pe.wait_ge(rk_done, B_TILES)
            for n in range(NT):
                for j in range(B_TILES):
                    ins = pe.matmul(bank[0][:, n * HEADS + 2 * j:n * HEADS + 2 * j + 2], sq[:, j, n * P:(n + 1) * P],
                                    pairsel[:], start=True, stop=True)
            ins.then_inc(bon_ps, 1)
            pe.wait_ge(rw_ready, B_TILES + 1)
            for g in range(16):
                arr, n = g // 4, g % 4
                if g >= 8:
                    pe.wait_ge(tok_a if g % 2 == 0 else tok_d, (g - 8) // 2 + 1)
                src = (rw[:, RA], rw[:, RB], rw[:, RK], yt0[:, 4:8])[arr]
                for j in range(B_TILES):
                    ins = pe.transpose(bank[g % 8][:, j * P:(j + 1) * P], src[:, j, n * P:(n + 1) * P], ident[:])
                ins.then_inc(tok_ps, 1)
            pe.wait_ge(tok_a, 8)
            pe.wait_ge(tok_d, 8)

            def rw_step(n, step, h):
                q = bank[4 * h:4 * h + 4]
                c = slice(n * P, (n + 1) * P)
                if step == "A":
                    if n > 0:
                        pe.wait_ge(rw_dve, nth(RW_DVE, n - 1, "Y", h))
                    for hd in range(4):
                        rows, j = slice(HD * (hd % 2), HD * (hd % 2) + HD), 2 * h + hd // 2
                        ar = rw[rows, RA:RR + 1, j, c]
                        pe.matmul(q[hd][:, 0:2 * P], rw[rows, RB, j, c], ar, start=True, stop=True)
                        ins = pe.matmul(q[hd][:, 2 * P:4 * P], rw[rows, RK, j, c], ar, start=True, stop=True)
                elif step == "AV":
                    pe.wait_ge(rw_dve, nth(RW_DVE, n, "A", h))
                    for hd in range(4):
                        col = (4 * h + hd) * HD
                        ins = pe.matmul(q[3][:, hd * HD:(hd + 1) * HD], mt[:, h, hd, 2, :], tok[:, V_TOK, n, col:col + HD],
                                        start=True, stop=True)
                elif step[0] == "T":
                    if step != "T0":
                        pe.wait_ge(rw_dve, nth(RW_DVE, n, "D" + step[1], h))
                    for hd in range(4):
                        ins = pe.transpose(q[0][:, hd * P:(hd + 1) * P], tt[:, h, hd, :], ident[:])
                elif step[0] == "P":
                    pe.wait_ge(rw_act, nth(RW_ACT, n, "T" + str(int(step[1]) - 1), h))
                    for hd in range(4):
                        ins = pe.matmul(q[1][:, hd * P:(hd + 1) * P], mt[:, h, hd, 0, :], tn[:, h, hd, :], start=True, stop=True)
                elif step[0] == "D":
                    pe.wait_ge(rw_act, nth(RW_ACT, n, "P" + step[1], h))
                    for hd in range(4):
                        ins = pe.matmul(q[2][:, hd * P:(hd + 1) * P], pp[:, h, hd, :], tt[:, h, hd, :], start=True, stop=True)
                elif step == "HG":
                    pe.wait_ge(rw_dve, nth(RW_DVE, n, "D6", h))
                    for hd in range(4):
                        col = (4 * h + hd) * HD
                        pe.matmul(q[0][:, hd * P:hd * P + HD], tt[:, h, hd, :], av[:, h, hd, :], start=True, stop=True)
                        ins = pe.matmul(q[0][:, hd * P + HD:(hd + 1) * P], tt[:, h, hd, :], tok[:, A_TOK, n, col:col + HD],
                                        start=True, stop=True)
                elif step == "R":
                    pe.wait_ge(rw_act, nth(RW_ACT, n, "HG", h))
                    for hd in range(4):
                        rows, jj, col = slice(HD * (hd % 2), HD * (hd % 2) + HD), hd // 2, (4 * h + hd) * HD
                        g, hh = hg[:, h, hd, HD:P], hg[:, h, hd, 0:HD]
                        pe.matmul(q[1][rows, jj * P:(jj + 1) * P], g, mt[:, h, hd, 1, :], start=True, stop=True)
                        pe.matmul(q[1][rows, 2 * P + jj * HD:2 * P + (jj + 1) * HD], g, tok[:, B_TOK, n, col:col + HD],
                                  start=True, stop=True)
                        pe.matmul(q[3][rows, 2 * P + jj * HD:2 * P + (jj + 1) * HD], tok[:, B_TOK, n, col:col + HD], hh,
                                  start=True, stop=False)
                        ins = pe.matmul(q[3][rows, 2 * P + jj * HD:2 * P + (jj + 1) * HD], tok[:, K_TOK, n, col:col + HD],
                                        tok[:, V_TOK, n, col:col + HD], start=False, stop=True)
                else:
                    pe.wait_ge(rw_dve, nth(RW_DVE, n, "R", h))
                    pe.wait_ge(rw_act, nth(RW_ACT, n, "R", h))
                    if n > 0:
                        pe.wait_ge(gn_out, n) if h == 0 else None
                        for jj in range(2 if n < NT - 1 else 0):
                            pe.matmul(q[3][:, jj * P:(jj + 1) * P], mbd[:, 2 * h + jj, :], zbd[:, 2 * h + jj, :],
                                      start=True, stop=True)
                    for jj in range(2):
                        if n > 0:
                            pe.matmul(q[2][:, jj * P:(jj + 1) * P], r2[:, h, jj, :], zbd[:, 2 * h + jj, :],
                                      start=True, stop=False, skip_group_check=True)
                        for e in range(2):
                            hd = 2 * jj + e
                            dst, col = q[2][:, hd * HD:(hd + 1) * HD], (4 * h + hd) * HD
                            pe.matmul(dst, mt[:, h, hd, 1, :], hg[:, h, hd, 0:HD], start=n == 0, stop=False,
                                      skip_group_check=True)
                            ins = pe.matmul(dst, mt[:, h, hd, 3, :], tok[:, V_TOK, n, col:col + HD], start=False,
                                            stop=True, skip_group_check=True)
                ins.then_inc(rw_pe, 1)

            def gn_transposes(n):
                pe.wait_ge(gn_pool, 3 * (n + 1))
                for j in range(B_TILES):
                    ins = pe.transpose(bank[3][:, j * P:(j + 1) * P], y_tok[:, j * P:(j + 1) * P], ident[:])
                ins.then_inc(gn_ps, 1)

            for n in range(NT):
                for step in RW_PE:
                    for h in range(2):
                        rw_step(n, step, h)
                    if step == "P6" and n > 0:
                        gn_transposes(n - 1)
            pe.wait_ge(rw_dve, nth(RW_DVE, NT - 1, "Y", 1))
            for j in range(B_TILES):
                pe.matmul(bank[4 + j][:], g2[:, j * P:(j + 1) * P], gate_in[:], start=True, stop=True).then_inc(gate_ps, 1)
            gn_transposes(NT - 1)
            pe.wait_ge(gated, B_TILES)

            out_projection(W_OUT0, yt_hi0, yt_lo0, 0)
            x_transposed(1)

            def mlp(base, layer, f0):
                first_slab(base, 2 * layer + 1, lambda u: pe.wait_ge(conv_d, layer * 5 * FT + 3 + u), w_pair)

                def up_tiles(s, i):
                    if True:
                        pe.wait_ge(lo_done, base + s + 1 + 2 * i)
                        hi, lo = w_pair(w_hi, base + s), w_pair(w_lo, base + s)
                        for u in range(2):
                            pe.wait_ge(conv_d, layer * 5 * FT + 5 * s + 3 + u + 10 * i)
                            for k in range(KT):
                                ins = three(bank[2 * s + u][:], hi[:, u, k, :], lo[:, u, k, :], xt_hi[:, k, :],
                                            xt_lo[:, k, :], k == 0, k == KT - 1)
                            ins.then_inc(half_slab, 1)

                up_tiles(1, 0)
                with pe.Fori(1, FT // 2) as i:
                    for s in range(2):
                        up_tiles(s, i)
                dn = base + FT
                pe.wait_ge(conv_d, 10 + (layer + 1) * 5 * FT)
                row_tiles(dn, 0, act_hi, act_lo, True, False, f0)
                with pe.Fori(0, (FT // ROWS - 3) // 2) as i:
                    for s in range(2):
                        row_tiles(dn + 1 + s, i, act_hi, act_lo, False, False, f0 + ROWS * (1 + s))
                for s in (FT // ROWS - 2, FT // ROWS - 1):
                    row_tiles(dn + s, 0, act_hi, act_lo, False, s == FT // ROWS - 1, f0 + ROWS * s)

            mlp(W_UP0, 0, KT)
            x_transposed(2)

            first_slab(W_IN1, 2, lambda c: pe.wait_ge(tile1_d, c + 1), w_cols)
            pe.wait_ge(lo_done, W_IN1 + 2)
            for c in range(2):
                pe.wait_ge(tile1_d, 3 + c)
                column_tile(W_IN1 + 1, c, bank[2 + c])
            for part in range(2):
                with pe.Fori(1 - part, 2) as i:
                    for s in range(2):
                        pe.wait_ge(lo_done, W_IN1 + 4 * part + s + 1 + 2 * i)
                        for c in range(2):
                            t = 2 * s + c
                            if part == 0:
                                pe.wait_ge(tile1_d, t + 1 + 4 * i)
                            elif t == 0:
                                pe.wait_ge(tile1_d, 12)
                                pe.wait_ge(tile1_a, t + 1 + 4 * i)
                            else:
                                pe.wait_ge(tile1_a, t + 1 + 4 * i)
                            column_tile(W_IN1 + s, c, bank[t][:])
            with pe.Fori(0, 2) as i:
                for s in range(2):
                    n = W_IN1 + 8 + s
                    pe.wait_ge(lo_done, n + 1 + 2 * i)
                    pe.wait_ge(tile1_d, 10 + 2 * s + 4 * i)
                    hi, lo = w_cols(w_hi, n), w_cols(w_lo, n)
                    for t in range(NT):
                        dst = bank[4 + 2 * s + t // 2][:, (t % 2) * COLS:(t % 2 + 1) * COLS]
                        for k in range(KT):
                            th, tl = xt_hi[:, k, t * P:(t + 1) * P], xt_lo[:, k, t * P:(t + 1) * P]
                            pe.matmul(dst, th, hi[:, k, :], start=k == 0, stop=False)
                            pe.matmul(dst, th, lo[:, k, :], start=False, stop=False)
                            ins = pe.matmul(dst, tl, hi[:, k, :], start=False, stop=k == KT - 1)
                        if t % 2:
                            ins.then_inc(half_slab, 1)
            pe.wait_ge(tile1_d, 20)
            pe.wait_ge(tile1_a, 12)
            pe.wait_ge(c_slopes, 1)

            def c_score(i, m):
                n, h = i // 8, i % 8
                return qc[m * HD:(m + 1) * HD, h, n * P:(n + 1) * P], kc[m * HD:(m + 1) * HD, h, 0:(n + 1) * P]

            attention(C_ITEMS, C_BANKS, lambda i: i // 8 + 1, c_s, c_exp, 1,
                      lambda i: (slope_id[:, i % 8, :], dist_c[:, (3 - i // 8) * P:4 * P]), c_p, c_t, c_tout, c_v, c_yout, c_y,
                      c_score, lambda i: [pc[:, i % 2, b * P:(b + 1) * P] for b in range(i // 8 + 1)],
                      lambda i: [(slice((i % 4) * P, (i % 4 + 1) * P),
                                  [(ptc[:, i % 2, b * P:(b + 1) * P], vc[:, b, (i % 8) * P:(i % 8 + 1) * P])
                                   for b in range(i // 8 + 1)])],
                      lambda g: yc[:, g % 2, :])
            pe.wait_ge(c_tout, len(C_BANKS))
            out_projection(W_OUT1, yt_hi1, yt_lo1, KT + FT)
            x_transposed(3)
            mlp(W_UP1, 1, 2 * KT + FT)

        @block.vector
        def _(dve):
            at = [0]

            def link(ins):
                at[0] += 1
                ins.then_inc(dve_at, 1)
                dve.wait_ge(dve_at, at[0])

            def x_low(r, n):
                if True:
                    for h in range(2):
                        dve.wait_ge(xt_h, 8 * r + 2 * n + h + 1)
                        view = (slice(None), slice(4 * h, 4 * h + 4), slice(n * P, (n + 1) * P))
                        dve.tensor_tensor(xt_lo[view], bank[2 * n + h].rearrange("p (k t) -> p k t", k=4),
                                          xt_hi[view].bitcast(F32), ALU.subtract).then_inc(xt_l, 1)

            def norm(l):
                gb = (ln_gb0, ln_gbf, ln_gb1, ln_gbf)[l]
                for stage, n in staggered(("statistics", "gain", "low")):
                    if stage == "statistics":
                        if n < NT - 1:
                            dve.wait_ge(acc_tile, (NT - 1) * l + n + 1)
                        else:
                            dve.wait_ge(half_slab, 2 * (W_UP0, W_IN1, W_UP1, W_END)[l])
                        for h in range(2):
                            xs = x_tok[:, n, h * 512:(h + 1) * 512]
                            link(dve.scalar_tensor_tensor(out=xs, in0=xs, scalar=ALPHA, in1=bank[2 * n + h][:],
                                                          op0=ALU.mult, op1=ALU.add))
                            ins = dve.bn_stats(bn2[:, n % 2, h, :], xs)
                            if h == 0:
                                ins.then_inc(dve_at, 1)
                                at[0] += 1
                            else:
                                link(ins)
                        link(dve.bn_aggr(mv[:, n, :], bn2[:, n % 2]))
                        dve.tensor_scalar(neg_mean[:, n:n + 1], mv[:, n, 0:1], -1.0, None, ALU.mult).then_inc(ln_sum, 1)
                        dve.tensor_scalar(mv[:, n, 1:2], mv[:, n, 1:2], LN_EPS, None, ALU.add).then_inc(ln_sum, 1)
                    elif stage == "gain":
                        if n == 0:
                            dve.wait_ge(gb_in[l], 32)
                        dve.wait_ge(ln_norm, l * NT + n + 1)
                        dve.tensor_tensor(x_tok[:, n, :], x_tok[:, n, :], gb[:, 0, :], ALU.mult).then_inc(ln_mul, 1)
                    elif l < 3:
                        x_low(l + 1, n)

            def row_tile(src, hi, lo, f, i, s, used):
                if used is not None:
                    dve.wait_ge(half_slab, used)
                dve.tensor_copy(hi[:, s, :], src).then_inc(act_split_h, 1)
                dve.wait_ge(act_split_h, f + 1 + 2 * i)
                dve.tensor_tensor(lo[:, s, :], src, hi[:, s, :].bitcast(F32), ALU.subtract).then_inc(act_split, 1)

            def attention(items, scores, dist, s_s, s_bias, s_max, s_exp, prev, sink, slope, s_v, finish_item, finish_group):
                for now in attention_steps(items):
                    for kind, i in now:
                        if kind == "S":
                            dve.wait_ge(s_s, i + 1)
                            if sink:
                                if i >= 3:
                                    dve.wait_ge(prev, transposed_banks(items)[("T", i - 3)] + 1)
                                for m in range(2):
                                    o, d, b = scores(i, m)
                                    dve.scalar_tensor_tensor(out=o, in0=d, scalar=-SLOPES[slope(i, m)], in1=b,
                                                             op0=ALU.mult, op1=ALU.add).then_inc(s_bias, 1)
                                dve.wait_ge(s_bias, 2 * i + 2)
                            both = scores(i, None)
                            if i > 0:
                                dve.wait_ge(s_max, i)
                            link(dve.tensor_reduce(maxes, both, AX_X, ALU.max))
                            if sink:
                                j = i % 4
                                link(dve.tensor_tensor(maxes, maxes, sinks[:, 2 * j:2 * j + 2], ALU.max))
                            ins = dve.tensor_scalar(neg_max[:, i % 2, :], maxes, -1.0, None, ALU.mult)
                            if sink:
                                link(ins)
                                ins = dve.tensor_tensor(sink_e[:, i % 2, :], sinks[:, 2 * j:2 * j + 2], neg_max[:, i % 2, :],
                                                        ALU.add)
                            ins.then_inc(s_max, 1)
                        elif kind == "C":
                            dve.wait_ge(s_exp, i + 1)
                            finish_item(i)
                        elif kind == "G":
                            dve.wait_ge(s_v, 4 * i + 4)
                            finish_group(i)

            dve.nop().then_inc(tile0_free, 4)
            dve.nop().then_inc(conv_d, 10)
            dve.nop().then_inc(tile1_d, 4)
            dve.wait_ge(consts_pool, 5)
            link(dve.tensor_copy(dist_f[:], iota_i[:, 0, :]))
            link(dve.scalar_tensor_tensor(out=dist_f[:], in0=dist_f[:], scalar=-1.0, in1=dist_f[:], op0=ALU.mult, op1=ALU.max))
            link(dve.tensor_copy(dist_a[:], dist_f[:, 2 * P:4 * P]))
            link(dve.memset(dist_f[0:HD, 4 * P - HD:4 * P], MASKED))
            link(dve.tensor_copy(dist_c[:], dist_f[:]))
            dve.memset(dist_a[0:HD, 0:HD], MASKED)
            dve.memset(dist_a[0:HD, 2 * P - HD:2 * P], MASKED)
            link(dve.memset(dist_a[HD:P, 0:P], MASKED))
            diff = iota_i[:, 1, 0:P]
            for q in range(4):
                link(dve.tensor_scalar(tri4[:, q, :], diff, 0.0, None, ALU.is_gt if q % 2 == 0 else ALU.is_ge))
            link(dve.tensor_scalar(ucum[:], diff, 0.0, DECAY_SCALE, ALU.is_ge, ALU.mult))
            link(dve.tensor_tensor(mask_t[:, 0, :], iota_i[:, 2, 0:P], iota_i[:, 3, 0:P], ALU.bitwise_xor))
            for k in range(LEVELS + 1):
                link(dve.tensor_scalar(mask_t[:, 1, :], mask_t[:, 0, :], k, None, ALU.logical_shift_right))
                link(dve.scalar_tensor_tensor(out=merge[:, k, :], in0=mask_t[:, 1, :], scalar=1.0, in1=tri4[:, 0, :],
                                              op0=ALU.is_equal, op1=ALU.mult))
            for n in range(NT):
                x_low(0, n)
            dve.wait_ge(par_ps, 1)
            link(dve.tensor_copy(chan[:], bank[6][:, 0:N_CHAN]))
            link(dve.tensor_scalar(one_minus[:], chan[:], -1.0, 1.0, ALU.mult, ALU.add))
            link(dve.tensor_scalar(sub_g[:], bank[6][:, N_CHAN:N_CHAN + 1], 1.0 - LAM_INIT, None, ALU.mult))
            dve.tensor_copy(conv[:].rearrange("p l c -> p (l c)"), bank[7][:, 0:DEPTH * N_CONV]).then_inc(consts_dve, 1)
            lam = lam_in[:].rearrange("p (a b) d -> p a b d", b=2)
            link(dve.tensor_tensor(lam_in[:, 0:4:2, :], lam[:, :, 0, :], lam[:, :, 1, :], ALU.mult))
            dve.tensor_reduce(lam_s[:, 0:2], lam_in[:, 0:4:2, :], AX_X, ALU.add).then_inc(consts_dve, 1)
            dve.wait_ge(squashed, 1)
            link(dve.memset(lam_c[:, 0:1], 1.0))
            dve.scalar_tensor_tensor(out=lam_c[:, 1:2], in0=lam_s[:, 3:4], scalar=-LAM_INIT, in1=lam_s[:, 2:3],
                                     op0=ALU.add, op1=ALU.subtract).then_inc(consts_dve, 1)

            def mix_target(t):
                if t == 0:
                    return wa[:]
                if t == 1:
                    return gate_in[:]
                j, which = (t - 2) % 4, (t - 2) // 4
                return (rw[:, RK, j, :], rw[:, RR, j, :], yt0[:, 4 + j, :])[which]

            def mix_row(t):
                return 12 + t if t < 2 else (4 + t - 2, t - 6, 8 + t - 10)[(t - 2) // 4]

            for t in range(MIX_COUNT):
                dve.wait_ge(mixed, t + 1)
                o, r = mix_target(t), mix_row(t)
                dve.scalar_tensor_tensor(out=o[:, 1:SEQ], in0=bank[t % 4][:, 0:SEQ - 1], scalar=chan[:, r:r + 1],
                                         in1=o[:, 1:SEQ], op0=ALU.mult, op1=ALU.add).then_inc(tile0_free, 1)
            for t in range(MIX_COUNT, MIX_COUNT + 4):
                dve.wait_ge(half_slab, t + 1)
                dve.tensor_scalar(qa[:, t - MIX_COUNT, :], bank[t % 4][:], HD ** -0.5, None, ALU.mult).then_inc(tile0_free, 1)
            dve.wait_ge(half_slab, 19)
            for kv in range(2):
                for e in range(2):
                    ins = dve.tensor_copy(kdup[e * HD:(e + 1) * HD, kv, :], bank[2][kv * HD:(kv + 1) * HD, :])
            ins.then_inc(tile0_free, 1)
            dve.wait_ge(half_slab, 20)
            dve.tensor_copy(va_ch[:], bank[3][:]).then_inc(tile0_free, 1)
            dve.wait_ge(va_ps, 1)
            dve.tensor_copy(va_tok[:].rearrange("p n c -> p (n c)"), bank[0][:]).then_inc(va_out, 1)

            def a_scores(i, m):
                w = P if i < 4 else 2 * P
                if m is None:
                    return sa[:, i % 3, :, 2 * P - w:2 * P]
                return sa[:, i % 3, m, 2 * P - w:2 * P], dist_a[:, 2 * P - w:2 * P], bank[(i % 2) * 2 + m][:, 0:w]

            def a_item(i):
                n, j = i // 4, i % 4
                link(dve.tensor_tensor(den[:, i % 2, :], den[:, i % 2, :], sink_e[:, i % 2, :], ALU.add))
                dve.reciprocal(rden[:, n % 2, 2 * j:2 * j + 2], den[:, i % 2, :]).then_inc(a_den, 1)

            def a_group(g):
                dve.wait_ge(a_den, 4 * g + 4)
                if g >= 2:
                    dve.wait_ge(a_t, A_BANKS[("Y", g - 2)] + 1)
                dve.tensor_tensor(ya[:, g % 2, :].rearrange("p (h c) -> p h c", h=HEADS),
                                  bank[6 + g % 2][:].rearrange("p (h c) -> p h c", h=HEADS),
                                  rden[:, g % 2, :].unsqueeze(2).to_broadcast([P, HEADS, HD]), ALU.mult).then_inc(a_y, 1)

            attention(A_ITEMS, a_scores, dist_a, a_s, a_bias, a_max, a_exp, a_t, True, lambda i, m: 2 * (i % 4) + m, a_v,
                      a_item, a_group)

            dve.wait_ge(a_tout, len(A_BANKS))
            for j in range(B_TILES):
                link(dve.tensor_scalar(rw[:, RA, j, :], rw[:, RK, j, :], chan[:, R_KK + j:R_KK + j + 1], None, ALU.mult))
                dve.tensor_tensor(sq[:, j, :], rw[:, RA, j, :], rw[:, RA, j, :], ALU.mult).then_inc(kk_sq, 1)
            for j in range(B_TILES):
                dve.wait_ge(cums, j + 1)
                ls = bank[j][:].rearrange("p (n t) -> p n t", n=NT)
                dve.tensor_scalar(cn[:, j, :], ls[:, :, P - 1], 0.5, None, ALU.mult).then_inc(centred, 1)
                dve.wait_ge(centred, 3 * j + 1)
                dve.tensor_scalar(epos[:, j, :, 0], cn[:, j, :], -1.0, None, ALU.mult).then_inc(centred, 1)
                dve.tensor_tensor(epos[:, j, :, 1:P + 1], ls, cn[:, j, :].unsqueeze(2).to_broadcast([P, NT, P]),
                                  ALU.subtract).then_inc(centred, 1)
            dve.tensor_tensor(zsc, cn[:, :, 0:NT - 1], cn[:, :, 1:NT], ALU.add).then_inc(centred, 1)
            dve.wait_ge(kk_ss, 1)
            dve.tensor_scalar(rs, bank[4][0:HEADS, :], 1e-24, None, ALU.max).then_inc(kk_max, 1)
            dve.wait_ge(kk_root, 1)
            dve.reciprocal(rs, rs).then_inc(kk_inv, 1)
            for j in range(B_TILES):
                c = lambda r: (chan[:, r + j:r + j + 1])
                A, K, KK, R = rw[:, RB, j, :], rw[:, RK, j, :], rw[:, RA, j, :], rw[:, RR, j, :]
                dve.wait_ge(lora_out, NT + j + 1)
                link(dve.tensor_scalar(sq[:, j, :], A, c(R_KA), one_minus[:, R_KA + j:R_KA + j + 1], ALU.mult, ALU.add))
                link(dve.tensor_tensor(K, K, sq[:, j, :], ALU.mult))
                dve.scalar_tensor_tensor(out=sq[:, j, :], in0=R, scalar=c(R_RK), in1=K, op0=ALU.mult, op1=ALU.mult) \
                    .then_inc(rk_done, 1)
                dve.wait_ge(kk_bc, j + 1)
                link(dve.tensor_tensor(KK, KK, bank[4 + j][:], ALU.mult))
                link(dve.tensor_tensor(A, A, KK, ALU.mult))
                dve.wait_ge(exps, j + 1)
                v4 = lambda t: t.rearrange("p (n t) -> p n t", n=NT)
                link(dve.tensor_tensor(v4(K), v4(K), eneg[:, j], ALU.mult))
                link(dve.tensor_tensor(v4(A), v4(A), eneg[:, j], ALU.mult))
                link(dve.tensor_tensor(v4(R), v4(R), epos[:, j, :, 1:P + 1], ALU.mult))
                dve.scalar_tensor_tensor(out=v4(KK), in0=v4(KK), scalar=-1.0, in1=epos[:, j, :, 0:P], op0=ALU.mult,
                                         op1=ALU.mult).then_inc(rw_ready, 1)
            dve.wait_ge(bon_ps, 1)
            dve.tensor_copy(bonus, bank[0][:, 0:NT * HEADS].rearrange("p (n h) -> p n h", n=NT)).then_inc(rw_ready, 1)
            for g in range(16):
                if g % 2:
                    dve.wait_ge(tok_ps, g + 1)
                    dve.tensor_copy(tok[:, g // 4, g % 4, :], bank[g % 8][:]).then_inc(tok_d, 1)

            def rw_step(n, step, h):
                q = bank[4 * h:4 * h + 4]
                dve.wait_ge(rw_pe, nth(RW_PE, n, step, h))
                if step == "A":
                    if n == 0:
                        dve.wait_ge(rw_init, h + 1)
                    for hd in range(4):
                        link(dve.copy_predicated(mt[:, h, hd].rearrange("p m t -> p (m t)"),
                                                 tri4[:].rearrange("p m t -> p (m t)"), q[hd][:]))
                    link(dve.tensor_copy(tt[:, h], ident[:].unsqueeze(1).to_broadcast([P, 4, P])))
                    ins = dve.copy_predicated(tt[:, h], merge[:, 0:1, :].to_broadcast([P, 4, P]), mt[:, h, :, 0, :])
                elif step[0] == "D":
                    k = int(step[1])
                    ins = dve.copy_predicated(tt[:, h], merge[:, k:k + 1, :].to_broadcast([P, 4, P]),
                                              q[2][:].rearrange("p (a t) -> p a t", a=4))
                elif step == "R":
                    dve.tensor_tensor(r2[:, h], q[1][:, 0:2 * P].rearrange("p (a t) -> p a t", a=2),
                                      rw[:, RR, 2 * h:2 * h + 2, n * P:(n + 1) * P], ALU.add)
                    for e in range(2):
                        rows = slice(e * HD, (e + 1) * HD)
                        ins = dve.tensor_tensor(mbd[rows, 2 * h:2 * h + 2, rows],
                                                q[1][rows, 2 * P:3 * P].rearrange("p (a t) -> p a t", a=2),
                                                ident[rows, rows].unsqueeze(1).to_broadcast([HD, 2, HD]), ALU.add)
                else:
                    if n > 0 and h == 0:
                        dve.wait_ge(gn_ps, n)
                    dve.wait_ge(rw_act, nth(RW_ACT, n, "R", h))
                    ins = dve.tensor_copy(y_tok[:, 4 * h * HD:4 * (h + 1) * HD], q[2][:, 0:2 * P])
                    if n < NT - 1:
                        nn = nst[:, 2 * h:2 * h + 2, :]
                        if n > 0:
                            for e in range(2):
                                rows = slice(e * HD, (e + 1) * HD)
                                link(dve.tensor_tensor(nn[rows], nn[rows],
                                                       q[3][:, 0:2 * P].rearrange("p (a c) -> p a c", a=2)[rows, :, rows],
                                                       ALU.add))
                        for e in range(2):
                            rows = slice(e * HD, (e + 1) * HD)
                            ins = dve.tensor_tensor(zbd[rows, 2 * h:2 * h + 2, rows], nn[rows],
                                                    zsc[rows, 2 * h:2 * h + 2, n:n + 1].to_broadcast([HD, 2, HD]), ALU.mult)
                ins.then_inc(rw_dve, 1)

            def group_norm(n, part):
                y8 = y_tok[:].rearrange("p (h c) -> p h c", h=HEADS)
                s8 = tok[:, A_TOK, n, :].rearrange("p (h c) -> p h c", h=HEADS)
                v8 = tok[:, V_TOK, n, :].rearrange("p (h c) -> p h c", h=HEADS)
                if part == 0:
                    dve.wait_ge(rw_dve, nth(RW_DVE, n, "Y", 1))
                    link(dve.tensor_reduce(gn_m, y8, AX_X, ALU.add))
                    link(dve.tensor_scalar(gn_m, gn_m, 1.0 / HD, None, ALU.mult))
                    dve.tensor_tensor(y8, y8, gn_m.unsqueeze(2).to_broadcast([P, HEADS, HD]), ALU.subtract) \
                        .then_inc(gn_dve, 1)
                elif part == 1:
                    dve.wait_ge(gn_pool, 3 * n + 1)
                    link(dve.tensor_reduce(gn_v, s8, AX_X, ALU.add))
                    dve.tensor_scalar(gn_v, gn_v, 1.0 / HD, GN_EPS, ALU.mult, ALU.add).then_inc(gn_dve, 1)
                elif part == 2:
                    dve.wait_ge(gn_pool, 3 * n + 2)
                    dve.tensor_tensor(y8, y8, gn_v.unsqueeze(2).to_broadcast([P, HEADS, HD]), ALU.mult).then_inc(gn_dve, 1)
                    dve.tensor_tensor(v8, v8, bonus[:, n, :].unsqueeze(2).to_broadcast([P, HEADS, HD]), ALU.mult) \
                        .then_inc(gn_dve, 1)

            dve.wait_ge(exps, B_TILES + 1)
            dve.wait_ge(consts_pool, 13)
            for n in range(NT):
                for step in RW_DVE:
                    for h in range(2):
                        rw_step(n, step, h)
                    if n > 0 and step in ("D1", "D2", "D3"):
                        group_norm(n - 1, int(step[1]) - 1)
            for part in range(3):
                group_norm(NT - 1, part)
            for j in range(B_TILES):
                dve.wait_ge(gate_ps, j + 1)
                dve.wait_ge(gn_out, NT)
                dve.tensor_tensor(yt0[:, 4 + j, :], yt0[:, 4 + j, :], bank[4 + j][:], ALU.mult).then_inc(gated, 1)

            def out_projection(base, yt, hi, lo, f0):
                dve.wait_ge(gated, B_TILES) if f0 == 0 else None
                for f in range(KT):
                    row_tile(yt[:, f, :], hi, lo, f0 + f, 0, f % 2, 2 * base + f - 1 if f >= 2 else None)

            def mlp(base, layer, f0):
                cw = conv[:, layer, :].rearrange("p (w u f) -> p w u f", w=4, u=2)
                with dve.Fori(0, FT // 2) as i:
                    for s in range(2):
                        done = 10 + layer * 5 * FT + 5 * s
                        for w, back in ((1, 1), (0, 2)):
                            for u, buf in enumerate((cu, cg)):
                                if w == 1:
                                    dve.wait_ge(conv_a, layer * 2 * FT + 2 * s + u + 1 + 4 * i)
                                else:
                                    dve.wait_ge(conv_d, done + u + 1 + 10 * i)
                                dve.scalar_tensor_tensor(out=buf[:, s, back:SEQ], in0=bank[2 * s + u][:, 0:SEQ - back],
                                                         scalar=cw[:, w, u, bass.ds(2 * i + s, 1)], in1=buf[:, s, back:SEQ],
                                                         op0=ALU.mult, op1=ALU.add).then_inc(conv_d, 1)
                        dve.wait_ge(silu_a, layer * FT + s + 1 + 2 * i)
                        dve.tensor_tensor(act_t[:, bass.ds(2 * i + s, 1), :].rearrange("p o t -> p (o t)"), cu[:, s, :],
                                          cg[:, s, :], ALU.mult).then_inc(conv_d, 1)
                for f in range(2):
                    dve.wait_ge(conv_d, 10 + (layer + 1) * 5 * FT)
                    row_tile(act_t[:, f, :], act_hi, act_lo, f0 + f, 0, f, None)
                with dve.Fori(0, FT // 2 - 1) as i:
                    for s in range(2):
                        src = act_t[:, bass.ds(2 * i + 2 + s, 1), :].rearrange("p o t -> p (o t)")
                        row_tile(src, act_hi, act_lo, f0 + 2 + s, i, s, 2 * (base + FT) + s + 1 + 2 * i)

            out_projection(W_OUT0, yt0, yt_hi0, yt_lo0, 0)
            norm(0)
            mlp(W_UP0, 0, KT)
            norm(1)

            with dve.Fori(0, 2) as i:
                for t in range(4):
                    dve.wait_ge(half_slab, 2 * W_IN1 + t + 1 + 4 * i)
                    dve.tensor_scalar(qc[:, bass.ds(4 * i + t, 1), :].rearrange("p o t -> p (o t)"), bank[t][:],
                                      HD ** -0.5, None, ALU.mult).then_inc(tile1_d, 1)
            with dve.Fori(0, 2) as i:
                for s in range(2):
                    for u in range(2):
                        dve.wait_ge(half_slab, 2 * W_IN1 + 16 + 2 * s + u + 1 + 4 * i)
                        dve.tensor_copy(vc[:, 2 * u:2 * u + 2, bass.ds(2 * COLS * i + COLS * s, COLS)],
                                        bank[4 + 2 * s + u][:].rearrange("p (n c) -> p n c", n=2)).then_inc(tile1_d, 1)

            for h in range(HEADS):
                ins = dve.tensor_scalar(slope_id[:, h, :], ident[:], -SLOPES[h], None, ALU.mult)
            ins.then_inc(c_slopes, 1)

            def c_scores(i, m):
                return bank_pair[i % 2][:, :, 0:P * (i // 8 + 1)]

            def c_item(i):
                w = P * (i // 8 + 1)
                link(dve.reciprocal(den[:, i % 2, :], den[:, i % 2, :]))
                link(dve.tensor_tensor(den[:, i % 2, :], den[:, i % 2, :], lam_c[:], ALU.mult))
                link(dve.tensor_scalar(sc[:, i % 2, 1, 0:w], sc[:, i % 2, 1, 0:w], den[:, i % 2, 1:2], None, ALU.mult))
                if i >= 2:
                    dve.wait_ge(c_t, C_BANKS[("T", i - 2)] + 1)
                dve.scalar_tensor_tensor(out=pc[:, i % 2, 0:w], in0=sc[:, i % 2, 0, 0:w], scalar=den[:, i % 2, 0:1],
                                         in1=sc[:, i % 2, 1, 0:w], op0=ALU.mult, op1=ALU.add).then_inc(c_p, 1)

            def c_group(g):
                if g >= 2:
                    dve.wait_ge(c_t, C_BANKS[("Y", g - 2)] + 1)
                y4 = yc[:, g % 2, :].rearrange("p (h c) -> p h c", h=4)
                dve.tensor_copy(yc[:, g % 2, :], bank[6 + g % 2][:]).then_inc(c_yout, 1)
                dve.wait_ge(c_yout, g + 1)
                dve.tensor_tensor(ysq[:], yc[:, g % 2, :], yc[:, g % 2, :], ALU.mult).then_inc(c_sq, 1)
                dve.wait_ge(c_sq, 3 * g + 1)
                dve.tensor_reduce(rms, ysq[:].rearrange("p (h c) -> p h c", h=4), AX_X, ALU.add).then_inc(c_sq, 1)
                dve.wait_ge(c_sq, 3 * g + 2)
                dve.tensor_scalar(rms, rms, 1.0 / P, SUBLN_EPS, ALU.mult, ALU.add).then_inc(c_sq, 1)
                dve.wait_ge(c_rms, g + 1)
                dve.tensor_tensor(y4, y4, rms.unsqueeze(2).to_broadcast([P, 4, P]), ALU.mult).then_inc(c_y, 1)

            attention(C_ITEMS, c_scores, None, c_s, None, c_max, c_exp, None, False, None, c_v,
                      c_item, c_group)
            dve.wait_ge(c_tout, len(C_BANKS))
            out_projection(W_OUT1, yt1, yt_hi1, yt_lo1, KT + FT)
            norm(2)
            mlp(W_UP1, 1, 2 * KT + FT)
            norm(3)


N_PARAM_DMAS = 18

_INS = ['x', 'ln_g', 'ln_b', 'ev_w_in', 'ev_sinks', 'ev_mu', 'ev_w0', 'ev_w2', 'ev_a0', 'ev_a2', 'ev_g2', 'ev_k_k', 'ev_k_a',
        'ev_r_k', 'ev_gn_g', 'ev_gn_b', 'ev_w_out', 'od_w_in', 'od_lam', 'od_subln_g', 'od_w_out',
        'ffn_w_up', 'ffn_conv_w', 'ffn_conv_b', 'ffn_w_down']
_OUTS = [((1, SEQ, D), 'float32')]


def kernel(**inputs):
    import numpy as _np
    import concourse.bacc as _bacc
    from concourse import mybir as _mybir
    from concourse.bass_utils import run_bass_kernel_spmd as _run

    nc = _bacc.Bacc("TRN2", target_bir_lowering=False, num_devices=1)
    arrays, args = {}, []
    for name in _INS:
        a = _np.ascontiguousarray(inputs[name])
        arrays[f"in_{name}_dram"] = a
        args.append(nc.dram_tensor(f"in_{name}_dram", a.shape, _mybir.dt.from_np(a.dtype), kind="ExternalInput").ap())
    for i, (shape, dtype) in enumerate(_OUTS):
        dt = _mybir.dt.from_np(_np.dtype(dtype))
        args.append(nc.dram_tensor(f"out_{i}_dram", shape, dt, kind="ExternalOutput").ap())
    encoder(nc, *args)
    r = _run(nc, [arrays], core_ids=[0])
    return r.results[0]["out_0_dram"]
```

```python
import math
from contextlib import ExitStack

import concourse.bass as bass
from concourse import mybir

ALU = mybir.AluOpType
ACT = mybir.ActivationFunctionType
F32 = mybir.dt.float32
F32R = mybir.dt.float32r
I32 = mybir.dt.int32
U8 = mybir.dt.uint8
AX_X = mybir.AxisListType.X

P = 128
SEQ = 512
NT = SEQ // P
D = 1024
KT = D // P
DEPTH = 2
HD = 64
HEADS = 8
A_Q = HEADS * HD
A_KV = 2 * HD
B_DIM = HEADS * HD
B_TILES = B_DIM // P
B0 = A_Q + 2 * A_KV
EVEN_IN = B0 + 3 * B_DIM + 256
MU_TILES = (EVEN_IN - B0) // P
C_QK = 1024
F = 2816
FT = F // P
ALPHA = (2.0 * DEPTH) ** 0.25
LN_EPS = 1e-5
GN_EPS = 64e-5
SUBLN_EPS = 1e-5
LAM_INIT = 0.8 - 0.6 * math.exp(-0.3)
MASKED = 1e30
DECAY_SCALE = -math.exp(-0.5)
SLOPES = [2.0 ** (-8.0 * (h + 1) / HEADS) for h in range(HEADS)]

SLAB = 2048
COLS = SLAB // KT
ROWS = SLAB // D
W_IN0 = 0
W_OUT0 = W_IN0 + EVEN_IN // COLS
W_UP0 = W_OUT0 + KT // ROWS
W_DN0 = W_UP0 + FT
W_IN1 = W_DN0 + FT // ROWS
W_OUT1 = W_IN1 + 3 * C_QK // COLS
W_UP1 = W_OUT1 + KT // ROWS
W_DN1 = W_UP1 + FT
W_END = W_DN1 + FT // ROWS
IN0_COLS = [B0 + 3 * B_DIM] + [B0 + B_DIM + COLS * s for s in range(2)] + [B0 + COLS * s for s in range(2)] \
    + [B0 + 2 * B_DIM + COLS * s for s in range(2)] + [COLS * s for s in range(2)] + [A_Q]

R_MU, R_A0, R_KK, R_KA, R_RK = 0, 14, 18, 22, 26
N_CHAN = 30
N_CONV = 4 * 2 * FT
CONV_HALF = N_CONV // 2

LEVELS = 6
RW_PE = ["A0", "A1", "AV", "T0"] + [s + str(k) for k in range(1, LEVELS) for s in ("P", "D", "T")] + ["P6", "D6", "HG", "R", "Y"]
RW_DVE = ["A0", "A1"] + [f"D{k}" for k in range(1, LEVELS + 1)] + ["R", "Y"]
RW_ACT = ["AV", "T0"] + [s + str(k) for k in range(1, LEVELS) for s in ("P", "T")] + ["P6", "HG", "R"]


TOK_GROUPS = 4 * NT
GN_BANK = [3] * (NT - 1) + [7]
GN_AFTER = (("D1", 0), ("D2", 1), ("D3", 2))


def nth(steps, n, step):
    return n * len(steps) + steps.index(step) + 1


def recurrence_steps():
    return [(n, step, h) for n in range(NT) for step in RW_PE for h in range(2)]


def attention_steps(items, group, others=0):
    steps = []
    for t in range(items + group[-1][1] - 3):
        now = []
        for kind, lag in (("S", 0), ("C", 1), ("T", 2), ("V", 3)):
            if 0 <= t - lag < items:
                now.append((kind, t - lag))
        if 0 <= t - 2 < others:
            now.append(("O", t - 2))
        for kind, lag in group:
            if t >= lag and (t - lag) % 4 == 0:
                now.append((kind, (t - lag) // 4))
        steps.append(now)
    return steps


def transposed_banks(items, group, others=0):
    order = [s for now in attention_steps(items, group, others) for s in now if s[0] in "TYO"]
    return {s: n for n, s in enumerate(order)}


def column_parts(n):
    return (slice(0, D),) if n < NT - 1 else (slice(0, D // 2), slice(D // 2, D))


def staggered(stages):
    return [(stage, t - lag) for t in range(2 * NT) for stage, lag in stages if 0 <= t - lag < NT]


def encoder(nc, x, ln_g, ln_b, ev_w_in, ev_sinks, ev_mu, ev_w0, ev_w2, ev_a0, ev_a2, ev_g2, ev_k_k, ev_k_a,
            ev_r_k, ev_gn_g, ev_gn_b, ev_w_out, od_w_in, od_lam, od_subln_g, od_w_out,
            ffn_w_up, ffn_conv_w, ffn_conv_b, ffn_w_down, out):
    with ExitStack() as ctx:
        def sb(name, shape, dt=F32, where=ctx):
            return where.enter_context(nc.sbuf_tensor(name, shape, dt))

        def sem(name):
            return ctx.enter_context(nc.semaphore(name))

        bank_pair = [ctx.enter_context(nc.psum_tensor(f"bank_pair{i}", [P, 2, 512], F32)) for i in range(4)]
        bank = [bank_pair[i // 2][:, i % 2, :] for i in range(8)]

        x_tok = sb("x_tok", [P, NT, D])
        w_raw = sb("w_raw", [P, 2, SLAB])
        w_hi = sb("w_hi", [P, 2, SLAB], F32R)
        w_lo = sb("w_lo", [P, 2, SLAB], F32R)
        ident = sb("ident", [P, P])
        dist_a = sb("dist_a", [P, 2 * P])
        dist_c = sb("dist_c", [P, 4 * P], F32R)
        tri4 = sb("tri4", [P, 4, P], U8)
        merge = sb("merge", [P, LEVELS + 1, P], U8)
        ucum = sb("ucum", [P, P])
        chan = sb("chan", [P, N_CHAN])
        one_minus = sb("one_minus", [P, N_CHAN])
        conv = sb("conv", [P, DEPTH, N_CONV])
        headsel = sb("headsel", [P, B_TILES, HEADS])
        headsel_t = sb("headsel_t", [HEADS, B_TILES, P])
        pairsel = sb("pairsel", [P, 2])
        sinks = sb("sinks", [P, HEADS])
        lam_c = sb("lam_c", [P, 2])
        sub_g = sb("sub_g", [P, 1])
        half_neg = sb("half_neg", [P, HEADS])
        w0_row = sb("w0_row", [1, B_DIM])
        ones_row = sb("ones_row", [1, P])
        small = sb("small", [P, 160])

        with ExitStack() as xs:
            xt_hi = sb("xt_hi", [P, KT, SEQ], F32R, xs)
            xt_lo = sb("xt_lo", [P, KT, SEQ], F32R, xs)
        tok = sb("tok", [P, 4, NT, B_DIM])
        A_TOK, B_TOK, K_TOK, V_TOK = range(4)

        with ExitStack() as m0:
            rw = sb("rw", [P, 4, B_TILES, SEQ], F32, m0)
            RA, RR, RB, RK = range(4)
            yt0 = sb("yt0", [P, KT, SEQ], F32, m0)
            wa = sb("wa", [P, SEQ], F32, m0)
            gate_in = sb("gate_in", [P, SEQ], F32, m0)
            w2a2 = sb("w2a2", [P, B_DIM], F32, m0)
            g2 = sb("g2", [P, B_DIM], F32, m0)
            gn_gb = sb("gn_gb", [P, 2, B_DIM], F32, m0)
            y_tok = sb("y_tok", [P, B_DIM], F32, m0)
            zbd = sb("zbd", [P, B_TILES, P], F32, m0)
            mbd = sb("mbd", [P, B_TILES, P], F32, m0)
            nst = sb("nst", [P, B_TILES, HD], F32, m0)
            with ExitStack() as u:
                prow = sb("prow", [P, 5, P], F32, u)
                lam_in = sb("lam_in", [P, 4, HD], F32, u)
                dist_f = sb("dist_f", [P, 4 * P], F32, u)
                iota_i = sb("iota_i", [P, 4, 512], I32, u)
                mask_t = sb("mask_t", [P, 3, P], I32, u)
            with ExitStack() as u:
                qa = sb("qa", [P, 4, SEQ], F32, u)
                kdup = sb("kdup", [P, 2, SEQ], F32, u)
                va_ch = sb("va_ch", [P, SEQ], F32, u)
                va_tok = sb("va_tok", [P, NT, P], F32, u)
                sa = sb("sa", [P, 3, 2, 2 * P], F32, u)
                pta = sb("pta", [P, 2, 512], F32, u)
                ya = sb("ya", [P, 2, 512], F32, u)
            with ExitStack() as u:
                epos = sb("epos", [P, B_TILES, NT, P + 1], F32, u)
                eneg = sb("eneg", [P, B_TILES, NT, P], F32, u)
                l_tok = sb("l_tok", [P, NT, B_DIM], F32, u)
                sq = sb("sq", [P, B_TILES, SEQ], F32, u)
            with ExitStack() as u:
                mt = sb("mt", [P, 2, 4, 4, P], F32, u)
                tt = sb("tt", [P, 2, 4, P], F32, u)
                tn = sb("tn", [P, 2, 4, P], F32, u)
                pp = sb("pp", [P, 2, 4, P], F32, u)
                av_a = sb("av_a", [P, 2, 4, P], F32, u)
                hg = pp
                r2 = tn
            with ExitStack() as u:
                ln_gb0 = sb("ln_gb0", [P, 2, D], F32, u)
                yt_hi0 = sb("yt_hi0", [P, 2, SEQ], F32R, u)
                yt_lo0 = sb("yt_lo0", [P, 2, SEQ], F32R, u)
        with ExitStack() as m1:
            act_t = sb("act_t", [P, FT, SEQ], F32, m1)
            act_hi = sb("act_hi", [P, 2, SEQ], F32R, m1)
            act_lo = sb("act_lo", [P, 2, SEQ], F32R, m1)
            cu = sb("cu", [P, 2, SEQ], F32, m1)
            cg = sb("cg", [P, 2, SEQ], F32, m1)
            ln_gbf = sb("ln_gbf", [P, 2, D], F32, m1)
        with ExitStack() as m2:
            qc = sb("qc", [P, HEADS, SEQ], F32, m2)
            kc = sb("kc", [P, HEADS, SEQ], F32, m2)
            slope_id = sb("slope_id", [P, HEADS, P], F32R, m2)
            vc = sb("vc", [P, NT, D], F32, m2)
            yt1 = sb("yt1", [P, KT, SEQ], F32, m2)
            pc = sb("pc", [P, 2, SEQ], F32, m2)
            ptc = sb("ptc", [P, 2, SEQ], F32, m2)
            yc = sb("yc", [P, 2, 512], F32, m2)
            ysq = sb("ysq", [P, 512], F32, m2)
            ln_gb1 = sb("ln_gb1", [P, 2, D], F32, m2)
            with ExitStack() as u:
                sc = sb("sc", [P, 2, 2, SEQ], F32, u)
            with ExitStack() as u:
                yt_hi1 = sb("yt_hi1", [P, 2, SEQ], F32R, u)
                yt_lo1 = sb("yt_lo1", [P, 2, SEQ], F32R, u)

        rs = y_tok[0:HEADS, :]

        neg_max = small[:, 0:4].rearrange("p (b m) -> p b m", b=2)
        den = small[:, 4:8].rearrange("p (b m) -> p b m", b=2)
        sink_e = small[:, 8:12].rearrange("p (b m) -> p b m", b=2)
        rden = small[:, 12:28].rearrange("p (b h) -> p b h", b=2)
        rms = small[:, 28:32]
        neg_mean = small[:, 32:36]
        shift = small[:, 36:40]
        mv = small[:, 56:64].rearrange("p (n s) -> p n s", n=4)
        rstd = small[:, 64:68]
        gn_m = small[:, 68:76]
        gn_v = small[:, 76:84]
        cn = small[:, 84:100].rearrange("p (j n) -> p j n", j=4)
        zsc = small[:, 100:112].rearrange("p (j n) -> p j n", j=4)
        bonus = small[:, 112:144].rearrange("p (n h) -> p n h", n=4)
        lam_s = small[:, 144:148]
        maxes = small[:, 148:150]
        bn2 = sb("bn2", [P, 2, 2, 6])

        par_rows = sem("par_rows")
        par_gn = sem("par_gn")
        x_in = [sem(f"x_in{n}") for n in range(NT)]
        w_landed = [sem(f"w_landed{i}") for i in range(2)]
        hi_done = sem("hi_done")
        first_half_hi = sem("first_half_hi")
        lo_done = sem("lo_done")
        half_slab = sem("half_slab")
        consts_pool = sem("consts_pool")
        consts_dve = sem("consts_dve")
        par_ps = sem("par_ps")
        xt_ps = sem("xt_ps")
        xt_h = sem("xt_h")
        xt_l = sem("xt_l")
        mixed = sem("mixed")
        tile0_free = sem("tile0_free")
        squashed = sem("squashed")
        va_ps = sem("va_ps")
        va_out = sem("va_out")
        a_s = sem("a_s"); a_bias = sem("a_bias"); a_max = sem("a_max"); a_exp = sem("a_exp"); a_den = sem("a_den")
        a_t = sem("a_t"); a_tout = sem("a_tout"); a_v = sem("a_v"); a_y = sem("a_y")
        c_s = sem("c_s"); c_max = sem("c_max"); c_exp = sem("c_exp"); c_p = sem("c_p")
        c_t = sem("c_t"); c_tout = sem("c_tout"); c_v = sem("c_v"); c_yout = sem("c_yout"); c_y = sem("c_y")
        c_slopes = sem("c_slopes"); c_sq = sem("c_sq"); c_square = sem("c_square"); c_rms = sem("c_rms")
        lora = sem("lora")
        lora_out = sem("lora_out")
        key_factor = sem("key_factor")
        cums = sem("cums")
        centred = sem("centred")
        exps = sem("exps")
        kk_sq = sem("kk_sq")
        kk_ss = sem("kk_ss")
        kk_max = sem("kk_max")
        kk_root = sem("kk_root")
        kk_inv = sem("kk_inv")
        kk_bc = sem("kk_bc")
        rk_done = sem("rk_done")
        bon_ps = sem("bon_ps")
        rw_ready = sem("rw_ready")
        rw_init = sem("rw_init")
        rw_pe, rw_dve, rw_act, tt_ident = [[sem(f"{e}{h}") for h in range(2)]
                                           for e in ("rw_pe", "rw_dve", "rw_act", "tt_ident")]
        gn_dve = sem("gn_dve"); gn_pool = sem("gn_pool"); gn_ps = sem("gn_ps"); gn_out = sem("gn_out")
        gate_ps = sem("gate_ps"); gated = sem("gated")
        act_split_h = sem("act_split_h")
        act_split = sem("act_split")
        ln_sum = sem("ln_sum")
        ln_rstd = sem("ln_rstd")
        ln_norm = sem("ln_norm")
        ln_last = sem("ln_last")
        ln_mul = sem("ln_mul")
        acc_tile = sem("acc_tile")
        ln_x = sem("ln_x")
        gb_in = [sem(f"gb_in{i}") for i in range(4)]
        conv_a = sem("conv_a")
        conv_d = sem("conv_d")
        silu_a = sem("silu_a")
        tile1_a = sem("tile1_a"); tile1_d = sem("tile1_d")
        dve_at = sem("dve_at")
        act_at = sem("act_at")
        pool_at = sem("pool_at")
        stored = sem("stored")

        MIX_COUNT = 14
        A_ITEMS, C_ITEMS = 16, 32
        A_GROUP = (("G", 7), ("Y", 9))
        C_GROUP = (("G", 6), ("H", 7), ("M", 8), ("Y", 9))
        A_BANKS, C_BANKS = transposed_banks(A_ITEMS, A_GROUP, TOK_GROUPS), transposed_banks(C_ITEMS, C_GROUP)

        def slot(n):
            return n % 2

        def w_cols(t, n):
            return t[:, slot(n), :].rearrange("p (k c) -> p k c", k=KT)

        def w_pair(t, n):
            return t[:, slot(n), :].rearrange("p (u k c) -> p u k c", u=2, k=KT)

        def w_rows(t, n):
            return t[:, slot(n), :].rearrange("p (r c) -> p r c", r=ROWS)

        block = ctx.enter_context(nc.Block())

        @block.sync
        def _(sp):
            def small_loads():
                rows = [(0, R_MU, ev_mu[0].rearrange("(t p) -> t p", p=P)),
                        (0, R_A0, ev_a0[0].rearrange("(t p) -> t p", p=P)),
                        (0, R_KK, ev_k_k[0].rearrange("(t p) -> t p", p=P)),
                        (0, R_KA, ev_k_a[0].rearrange("(t p) -> t p", p=P)),
                        (0, R_RK, ev_r_k[0].rearrange("(t e) d -> t (e d)", e=2)),
                        (0, N_CHAN, od_subln_g)]
                for k, r0, src in rows:
                    sp.dma_start(prow[r0:r0 + src.shape[0], k, :], src).then_inc(par_rows, 16)
                n_rows = len(rows)
                for l in range(DEPTH):
                    src = ffn_conv_w[l].rearrange("w (t p) -> (w t) p", p=P)
                    sp.dma_start(prow[0:CONV_HALF, 1 + 2 * l, :], src[0:CONV_HALF]).then_inc(par_rows, 16)
                    sp.dma_start(prow[0:3 * 2 * FT - CONV_HALF, 2 + 2 * l, :], src[CONV_HALF:3 * 2 * FT]).then_inc(par_rows, 16)
                    sp.dma_start(prow[3 * 2 * FT - CONV_HALF:CONV_HALF, 2 + 2 * l, :],
                                  ffn_conv_b[l].rearrange("(t p) -> t p", p=P)).then_inc(par_rows, 16)
                    n_rows += 3
                sp.dma_start(w2a2[0:HD, :], ev_w2[0]).then_inc(par_rows, 16)
                sp.dma_start(w2a2[HD:P, :], ev_a2[0]).then_inc(par_rows, 16)
                sp.dma_start(g2[:], ev_g2[0]).then_inc(par_rows, 16)
                sp.dma_start(w0_row[:], ev_w0).then_inc(par_rows, 16)
                sp.dma_start(sinks[:], ev_sinks[0].partition_broadcast(P)).then_inc(par_rows, 16)
                sp.dma_start(lam_in[:], od_lam[0].partition_broadcast(P)).then_inc(par_rows, 16)
                n_rows += 6
                assert n_rows == N_PARAM_DMAS
                sp.dma_start(gn_gb[:, 0, :], ev_gn_g[0].partition_broadcast(P)).then_inc(par_gn, 16)
                sp.dma_start(gn_gb[:, 1, :], ev_gn_b[0].partition_broadcast(P)).then_inc(par_gn, 16)

            in0 = ev_w_in[0].rearrange("(k p) c -> p k c", p=P)
            for s, c0 in enumerate(IN0_COLS):
                if s == 1:
                    sp.wait_ge(x_in[2], 16)
                if s == 2:
                    small_loads()
                if s >= 2:
                    sp.wait_ge(lo_done, s - 1)
                for h in range(2):
                    sp.dma_start(w_cols(w_raw, s)[:, 4 * h:4 * h + 4, :], in0[:, 4 * h:4 * h + 4, c0:c0 + COLS]) \
                        .then_inc(w_landed[slot(s)], 16)

            def rows_slab(base, w, n0, i, s):
                n = base + n0 + s
                sp.wait_ge(lo_done, n - 1 + 2 * i)
                for r in range(ROWS):
                    sp.dma_start(w_rows(w_raw, n)[:, r, :], w[bass.ds((2 * i + n0 + s) * ROWS * P + r * P, P), :]) \
                        .then_inc(w_landed[slot(n)], 16)

            def out_rows(base, w):
                for s in range(KT // ROWS):
                    rows_slab(base, w, s, 0, 0)

            def up(base, w):
                wv = w.rearrange("(k p) c -> p k c", p=P)
                with sp.Fori(0, FT // 2) as i:
                    for s in range(2):
                        sp.wait_ge(lo_done, base + s - 1 + 2 * i)
                        for u in range(2):
                            sp.dma_start(w_pair(w_raw, base + s)[:, u], wv[:, :, bass.ds(i * 2 * P + s * P + u * F, P)]) \
                                .then_inc(w_landed[slot(base + s)], 16)

            def down(base, w):
                with sp.Fori(0, (FT // ROWS) // 2) as i:
                    for s in range(2):
                        rows_slab(base, w, 0, i, s)
                rows_slab(base, w, FT // ROWS - 1, 0, 0)

            out_rows(W_OUT0, ev_w_out[0])
            up(W_UP0, ffn_w_up[0])
            down(W_DN0, ffn_w_down[0])
            in1 = od_w_in[0].rearrange("(k p) c -> p k c", p=P)
            with sp.Fori(0, (W_OUT1 - W_IN1) // 2) as i:
                for s in range(2):
                    sp.wait_ge(lo_done, W_IN1 + s - 1 + 2 * i)
                    for h in range(2):
                        sp.dma_start(w_cols(w_raw, W_IN1 + s)[:, 4 * h:4 * h + 4, :],
                                     in1[:, 4 * h:4 * h + 4, bass.ds(i * 2 * COLS + s * COLS, COLS)]) \
                            .then_inc(w_landed[slot(W_IN1 + s)], 16)
            out_rows(W_OUT1, od_w_out[0])
            up(W_UP1, ffn_w_up[1])
            down(W_DN1, ffn_w_down[1])
            for n in range(NT):
                sp.wait_ge(ln_x, 3 * NT + n + 1)
                if n == NT - 1:
                    sp.wait_ge(ln_last, DEPTH * 2)
                sp.dma_start(out[0, n * P:(n + 1) * P, :], x_tok[:, n, :]).then_inc(stored, 16)
            sp.wait_ge(stored, 16 * NT)

        @block.gpsimd
        def _(pool):
            at = [0]

            def link(ins):
                at[0] += 1
                ins.then_inc(pool_at, 1)
                pool.wait_ge(pool_at, at[0])

            def split(n, i=0):
                pool.wait_ge(hi_done, n + 1 + 2 * i)
                pool.tensor_tensor(w_lo[:, slot(n), :], w_raw[:, slot(n), :], w_hi[:, slot(n), :].bitcast(F32),
                                   ALU.subtract).then_inc(lo_done, 1)

            def norm_round(l):
                gb = (ln_gb0, ln_gbf, ln_gb1, ln_gbf)[l]
                for stage, n in staggered((("scale", 0), ("add", 1))):
                    if stage == "scale":
                        pool.wait_ge(ln_sum, 2 * (l * NT + n + 1))
                        link(pool.tensor_tensor(rstd[:, n:n + 1], mv[:, n, 1:2], half_neg[:, 0:1], ALU.pow))
                        pool.tensor_tensor(shift[:, n:n + 1], neg_mean[:, n:n + 1], rstd[:, n:n + 1], ALU.mult) \
                            .then_inc(ln_rstd, 1)
                    else:
                        if n == 0:
                            pool.wait_ge(gb_in[l], 32)
                        pool.wait_ge(ln_mul, l * (NT + 1) + n + 1)
                        cols = slice(0, D if n < NT - 1 else D // 2)
                        pool.tensor_tensor(x_tok[:, n, cols], x_tok[:, n, cols], gb[:, 1, cols], ALU.add).then_inc(ln_x, 1)

            pool.memset(ident[:], 0.0).then_inc(pool_at, 1)
            pool.memset(headsel[:], 1.0).then_inc(pool_at, 1)
            pool.memset(headsel_t[:], 1.0).then_inc(pool_at, 1)
            pool.memset(pairsel[:], 0.0).then_inc(pool_at, 1)
            at[0] = 4
            pool.wait_ge(pool_at, 4)
            pool.affine_select(out=ident[:], in_=ident[:], compare_op=ALU.not_equal, fill=1.0, base=0,
                               pattern=[[-1, P]], channel_multiplier=1).then_inc(consts_pool, 1)
            pool.iota(iota_i[:, 0, :], [[-1, 4 * P]], base=3 * P, channel_multiplier=1).then_inc(consts_pool, 1)
            pool.iota(iota_i[:, 1, 0:P], [[1, P]], base=0, channel_multiplier=-1).then_inc(consts_pool, 1)
            pool.iota(iota_i[:, 2, 0:P], [[1, P]], base=0, channel_multiplier=0).then_inc(consts_pool, 1)
            pool.iota(iota_i[:, 3, 0:P], [[0, P]], base=0, channel_multiplier=1).then_inc(consts_pool, 1)
            link(pool.affine_select(out=headsel[:], in_=headsel[:], compare_op=ALU.is_ge, fill=0.0, base=0,
                                    pattern=[[P, B_TILES], [-HD, HEADS]], channel_multiplier=1))
            pool.affine_select(out=headsel[:], in_=headsel[:], compare_op=ALU.is_ge, fill=0.0, base=HD - 1,
                               pattern=[[-P, B_TILES], [HD, HEADS]], channel_multiplier=-1).then_inc(consts_pool, 1)
            link(pool.affine_select(out=headsel_t[:], in_=headsel_t[:], compare_op=ALU.is_ge, fill=0.0, base=0,
                                    pattern=[[P, B_TILES], [1, P]], channel_multiplier=-HD))
            pool.affine_select(out=headsel_t[:], in_=headsel_t[:], compare_op=ALU.is_ge, fill=0.0, base=HD - 1,
                               pattern=[[-P, B_TILES], [-1, P]], channel_multiplier=HD).then_inc(consts_pool, 1)
            pool.memset(pairsel[0:HD, 0:1], 1.0).then_inc(consts_pool, 1)
            pool.memset(pairsel[HD:P, 1:2], 1.0).then_inc(consts_pool, 1)
            pool.wait_ge(consts_pool, 9)
            pool.memset(half_neg[:], -0.5).then_inc(consts_pool, 1)
            pool.memset(ones_row[:], 1.0).then_inc(consts_pool, 1)
            pool.memset(zbd[:], 0.0).then_inc(consts_pool, 1)
            pool.memset(mbd[:], 0.0).then_inc(consts_pool, 1)

            half = slice(0, SLAB // 2)
            pool.wait_ge(first_half_hi, 1)
            pool.tensor_tensor(w_lo[:, 0, half], w_raw[:, 0, half], w_hi[:, 0, half].bitcast(F32), ALU.subtract)
            half = slice(SLAB // 2, SLAB)
            pool.wait_ge(hi_done, 1)
            pool.tensor_tensor(w_lo[:, 0, half], w_raw[:, 0, half], w_hi[:, 0, half].bitcast(F32), ALU.subtract) \
                .then_inc(lo_done, 1)
            for n in range(1, W_UP0):
                split(n)
                if n == W_OUT0 + 1:
                    for h in range(2):
                        pool.wait_ge((a_s, a_v)[h], A_ITEMS)
                        pool.memset(mt[:, h], 0.0).then_inc(rw_init, 1)
                    for c in range(NT):
                        pool.wait_ge(gn_dve, 4 * c + 1)
                        pool.tensor_tensor(tok[:, A_TOK, c, :], y_tok[:], y_tok[:], ALU.mult).then_inc(gn_pool, 1)
                        pool.wait_ge(gn_dve, 4 * c + 2)
                        pool.tensor_tensor(gn_v, gn_v, half_neg[:], ALU.pow).then_inc(gn_pool, 1)
                        pool.wait_ge(gn_dve, 4 * c + 3)
                        if c == 0:
                            pool.wait_ge(par_gn, 32)
                        link(pool.tensor_tensor(y_tok[:], y_tok[:], gn_gb[:, 0, :], ALU.mult))
                        link(pool.tensor_tensor(y_tok[:], y_tok[:], gn_gb[:, 1, :], ALU.add))
                        pool.wait_ge(gn_dve, 4 * c + 4)
                        pool.tensor_tensor(y_tok[:], y_tok[:], tok[:, V_TOK, c, :], ALU.add).then_inc(gn_pool, 1)
            split(W_UP0)
            norm_round(0)
            split(W_UP0 + 1)
            with pool.Fori(0, (W_IN1 + 1 - W_UP0 - 2) // 2) as i:
                split(W_UP0 + 2, i)
                split(W_UP0 + 3, i)
            norm_round(1)
            split(W_IN1 + 1)
            with pool.Fori(0, (W_OUT1 - W_IN1 - 2) // 2) as i:
                split(W_IN1 + 2, i)
                split(W_IN1 + 3, i)
            split(W_OUT1)
            split(W_OUT1 + 1)
            for g in range(C_ITEMS // 4):
                pool.wait_ge(c_yout, g + 1)
                pool.tensor_tensor(ysq[:], yc[:, g % 2, :], yc[:, g % 2, :], ALU.mult).then_inc(c_square, 1)
                pool.wait_ge(c_sq, 2 * g + 2)
                pool.tensor_tensor(rms, rms, half_neg[:, 0:4], ALU.pow).then_inc(c_rms, 1)
            for n in range(W_OUT1 + 2, W_UP1 + 1):
                split(n)
            norm_round(2)
            split(W_UP1 + 1)
            with pool.Fori(0, (W_END - W_UP1 - 3) // 2) as i:
                split(W_UP1 + 2, i)
                split(W_UP1 + 3, i)
            split(W_END - 1)
            norm_round(3)

        @block.scalar
        def _(act):
            at = [0]

            def link(ins):
                at[0] += 1
                ins.then_inc(act_at, 1)
                act.wait_ge(act_at, at[0])

            def split(n, i=0, first=False):
                act.wait_ge(w_landed[slot(n)], 32 * (n // 2 + 1) + 32 * i)
                if not first:
                    act.wait_ge(half_slab, 2 * (n - 1) + 4 * i)
                act.activation(w_hi[:, slot(n), :], w_raw[:, slot(n), :], ACT.Copy).then_inc(hi_done, 1)

            def x_high(r, n):
                for h in range(2):
                    act.wait_ge(xt_ps, 8 * r + 2 * n + h + 1)
                    act.activation(xt_hi[:, 4 * h:4 * h + 4, n * P:(n + 1) * P],
                                   bank[2 * n + h].rearrange("p (k t) -> p k t", k=4), ACT.Copy).then_inc(xt_h, 1)

            def norm(l):
                for stage, n in staggered((("normalise", 0), ("high", 2))):
                    if stage == "normalise":
                        act.wait_ge(ln_rstd, l * NT + n + 1)
                        for cols in column_parts(n):
                            act.activation(x_tok[:, n, cols], x_tok[:, n, cols], ACT.Identity, bias=shift[:, n:n + 1],
                                           scale=rstd[:, n:n + 1]).then_inc(ln_norm, 1)
                    elif stage == "high" and l < 3:
                        x_high(l + 1, n)

            def load_gb(l, gb):
                act.dma_start(gb[:, 0, :], ln_g[l // 2, l % 2, :].partition_broadcast(P)).then_inc(gb_in[l], 16)
                act.dma_start(gb[:, 1, :], ln_b[l // 2, l % 2, :].partition_broadcast(P)).then_inc(gb_in[l], 16)

            def attention(items, banks, tiles, s_max, s_exp, s_t, s_tout, scores, probs, pt, sink,
                          target, scale, others=0):
                for now in attention_steps(items, C_GROUP if others == 0 else A_GROUP, others):
                    for kind, i in now:
                        if kind == "S":
                            act.wait_ge(s_max, i + 1)
                            width = tiles(i)
                            for m in range(2):
                                ins = act.activation(probs(i, m, width), scores(i, m, width), ACT.Exp,
                                                     bias=neg_max[:, i % 2, m:m + 1], accum_out=den[:, i % 2, m:m + 1])
                                if m == 1 and not sink:
                                    ins.then_inc(s_exp, 1)
                            if sink:
                                act.activation(sink_e[:, i % 2, :], sink_e[:, i % 2, :], ACT.Exp).then_inc(s_exp, 1)
                        elif kind == "G" and not sink:
                            act.wait_ge(c_v, 4 * i + 4)
                            if i >= 2:
                                act.wait_ge(c_t, C_BANKS[("Y", i - 2)] + 1)
                            act.activation(yc[:, i % 2, :], bank[6 + i % 2][:], ACT.Copy).then_inc(c_yout, 1)
                        elif kind in "TYO":
                            use = banks[(kind, i)]
                            act.wait_ge(s_t, use + 1)
                            if kind == "T":
                                nb = tiles(i) // P * (2 if sink else 1)
                                act.activation(pt[:, i % 2, 0:nb * P], bank[4 + use % 2][:, 0:nb * P], ACT.Copy) \
                                    .then_inc(s_tout, 1)
                            elif kind == "O":
                                act.activation(tok[:, i // NT, i % NT, :], bank[4 + use % 2], ACT.Copy).then_inc(s_tout, 1)
                            else:
                                src = bank[4 + use % 2][:].rearrange("p (c t) -> p c t", c=4)
                                if scale is None:
                                    act.activation(target(i), src, ACT.Copy).then_inc(s_tout, 1)
                                else:
                                    act.activation(target(i), src, ACT.Copy, scale=scale).then_inc(s_tout, 1)

            act.nop().then_inc(tile1_a, 4)
            for n in range(NT):
                act.dma_start(x_tok[:, n, :], x[0, n * P:(n + 1) * P, :]).then_inc(x_in[n], 16)
            for n in range(NT):
                x_high(0, n)
                if n < 2:
                    act.wait_ge(w_landed[0], 32)
                    cols = slice(n * SLAB // 2, (n + 1) * SLAB // 2)
                    act.activation(w_hi[:, 0, cols], w_raw[:, 0, cols], ACT.Copy).then_inc((first_half_hi, hi_done)[n], 1)
            split(1, first=True)
            act.wait_ge(consts_dve, 2)
            act.activation(lam_s[:, 2:4], lam_s[:, 0:2], ACT.Exp).then_inc(squashed, 1)

            def mix_target(t):
                if t == 0:
                    return wa[:]
                if t == 1:
                    return gate_in[:]
                j, which = (t - 2) % 4, (t - 2) // 4
                return (rw[:, RK, j, :], rw[:, RR, j, :], yt0[:, 4 + j, :])[which]

            def mix_row(t):
                return 12 + t if t < 2 else (4 + t - 2, t - 6, 8 + t - 10)[(t - 2) // 4]

            act.wait_ge(consts_dve, 3)
            for s in range(W_OUT0):
                for c in range(2):
                    t = 2 * s + c
                    if t < MIX_COUNT:
                        act.wait_ge(half_slab, t + 1)
                        r = mix_row(t)
                        act.activation(mix_target(t), bank[t % 4][:], ACT.Copy, scale=one_minus[:, r:r + 1]).then_inc(mixed, 1)
                split(s + 2)
                if s == 0:
                    act.wait_ge(tile0_free, 4 + 2)
                    act.activation(wa[0:HD, :], wa[0:HD, :], ACT.Tanh).then_inc(squashed, 1)
                    act.activation(gate_in[:], gate_in[:], ACT.Sigmoid).then_inc(squashed, 1)
                elif s == 1:
                    for n in range(NT):
                        act.wait_ge(lora, n + 1)
                        act.activation(l_tok[:, n, :], bank[4 + n][:], ACT.Sigmoid).then_inc(lora_out, 1)
                elif s == 3:
                    for j in range(B_TILES):
                        act.wait_ge(centred, 3 * j + 3)
                        link(act.activation(eneg[:, j], epos[:, j, :, 1:P + 1], ACT.Exp, scale=-1.0))
                        act.activation(epos[:, j], epos[:, j], ACT.Exp).then_inc(exps, 1)
                    act.wait_ge(centred, 3 * B_TILES + 1)
                    act.activation(zsc, zsc, ACT.Exp).then_inc(exps, 1)
                elif s == 4:
                    act.wait_ge(kk_max, 1)
                    act.activation(rs, rs, ACT.Sqrt).then_inc(kk_root, 1)
                    for j in range(B_TILES):
                        act.wait_ge(lora, NT + j + 1)
                        act.activation(rw[:, RB, j, :], bank[4 + j][:], ACT.Sigmoid, bias=chan[:, R_A0 + j:R_A0 + j + 1]) \
                            .then_inc(lora_out, 1)
                        act.wait_ge(lora_out, NT + j + 1)
                        act.activation(sq[:, j, :], rw[:, RB, j, :], ACT.Identity, scale=chan[:, R_KA + j:R_KA + j + 1],
                                       bias=one_minus[:, R_KA + j:R_KA + j + 1]).then_inc(key_factor, 1)

            attention(A_ITEMS, A_BANKS, lambda i: P if i < 4 else 2 * P, a_max, a_exp, a_t, a_tout,
                      scores=lambda i, m, w: sa[:, i % 3, m, 2 * P - w:2 * P],
                      probs=lambda i, m, w: sa[:, i % 3, m, 2 * P - w:2 * P], pt=pta, sink=True,
                      target=lambda g: yt0[:, 0:4, g * P:(g + 1) * P], scale=None, others=TOK_GROUPS)

            def rw_step(n, step, h):
                act.wait_ge(rw_pe[h], nth(RW_PE, n, step))
                if step == "AV":
                    act.activation(av_a[:, h, :, HD:P], tok[:, A_TOK, n, 4 * h * HD:4 * (h + 1) * HD]
                                   .rearrange("p (a c) -> p a c", a=4), ACT.Copy)
                    dst, src = av_a[:, h, :, 0:HD], bank[4 * h + 3][:, 0:4 * HD].rearrange("p (a c) -> p a c", a=4)
                elif step[0] == "T":
                    dst, src = tn[:, h], bank[4 * h][:].rearrange("p (a c) -> p a c", a=4)
                elif step[0] == "P":
                    dst, src = pp[:, h], bank[4 * h + 1][:].rearrange("p (a c) -> p a c", a=4)
                elif step == "HG":
                    dst, src = hg[:, h], bank[4 * h][:].rearrange("p (a c) -> p a c", a=4)
                else:
                    dst = nst[:, 2 * h:2 * h + 2, :]
                    src = bank[4 * h + 3][:, 2 * P:3 * P].rearrange("p (a c) -> p a c", a=2)
                act.activation(dst, src, ACT.Copy).then_inc(rw_act[h], 1)
                if step == "R" and n < NT - 1:
                    t_from_identity(h)

            def t_from_identity(h):
                act.activation(tt[:, h], ident[:].unsqueeze(1).to_broadcast([P, 4, P]), ACT.Copy).then_inc(tt_ident[h], 1)

            def gn_transposed(n):
                act.wait_ge(gn_ps, n + 1)
                act.activation(yt0[:, 4:8, n * P:(n + 1) * P], bank[GN_BANK[n]].rearrange("p (c t) -> p c t", c=4),
                               ACT.Copy).then_inc(gn_out, 1)

            act.wait_ge(a_tout, len(A_BANKS))
            for h in range(2):
                t_from_identity(h)
            for n, step, h in recurrence_steps():
                if step in RW_ACT:
                    rw_step(n, step, h)
                if step == "P6" and h == 0 and n > 0:
                    gn_transposed(n - 1)
            gn_transposed(NT - 1)
            load_gb(0, ln_gb0)

            def out_projection(base):
                for s in range(KT // ROWS - 1):
                    split(base + s + 2)

            out_projection(W_OUT0)
            norm(0)
            split(W_UP0 + 1)
            load_gb(1, ln_gbf)

            def mlp(base, layer, last):
                cw = conv[:, layer, :].rearrange("p (w u f) -> p w u f", w=4, u=2)
                with act.Fori(0, FT // 2) as i:
                    for s in range(2):
                        for u, buf in enumerate((cu, cg)):
                            act.wait_ge(half_slab, 2 * (base + s) + u + 1 + 4 * i)
                            act.wait_ge(conv_d, layer * 5 * FT + 5 * s + 5 + 10 * i)
                            act.activation(buf[:, s, :], bank[2 * s + u][:], ACT.Identity,
                                           bias=cw[:, 3, u, bass.ds(2 * i + s, 1)],
                                           scale=cw[:, 2, u, bass.ds(2 * i + s, 1)]).then_inc(conv_a, 1)
                        split(base + 2 + s, i)
                        act.wait_ge(conv_d, 10 + layer * 5 * FT + 5 * s + 4 + 10 * i)
                        act.activation(cg[:, s, :], cg[:, s, :], ACT.Silu).then_inc(silu_a, 1)
                n_down = FT // ROWS - (2 if last else 0)
                with act.Fori(0, n_down // 2) as i:
                    split(base + FT + 2, i)
                    split(base + FT + 3, i)
                if n_down % 2 and last:
                    split(base + FT + 2 + n_down - 1)

            mlp(W_UP0, 0, False)
            norm(1)
            split(W_IN1 + 1)
            load_gb(2, ln_gb1)

            with act.Fori(0, 2) as i:
                for s in range(2):
                    split(W_IN1 + 2 + s, i)
            with act.Fori(0, 2) as i:
                for s in range(2):
                    for c in range(2):
                        act.wait_ge(half_slab, 2 * W_IN1 + 8 + 2 * s + c + 1 + 4 * i)
                        act.activation(kc[:, bass.ds(4 * i + 2 * s + c, 1), :].rearrange("p o t -> p (o t)"),
                                       bank[2 * s + c][:], ACT.Copy).then_inc(tile1_a, 1)
                    split(W_IN1 + 6 + s, i)
            with act.Fori(0, 2) as i:
                for s in range(2):
                    split(W_IN1 + 10 + s, i)

            attention(C_ITEMS, C_BANKS, lambda i: P * (i // 8 + 1), c_max, c_exp, c_t, c_tout,
                      scores=lambda i, m, w: bank[(i % 2) * 2 + m][:, 0:w], probs=lambda i, m, w: sc[:, i % 2, m, 0:w],
                      pt=ptc, sink=False,
                      target=lambda g: yt1[:, 4 * (g % 2):4 * (g % 2) + 4, (g // 2) * P:(g // 2 + 1) * P],
                      scale=sub_g[:, 0:1])
            out_projection(W_OUT1)
            norm(2)
            split(W_UP1 + 1)
            load_gb(3, ln_gbf)
            mlp(W_UP1, 1, True)
            norm(3)

        @block.tensor
        def _(pe):
            def three(psum, hi, lo, rhi, rlo, start, stop):
                pe.matmul(psum, hi, rhi, start=start, stop=False)
                pe.matmul(psum, hi, rlo, start=False, stop=False)
                return pe.matmul(psum, lo, rhi, start=False, stop=stop)

            def x_transposed(r):
                for n in range(NT):
                    if r == 0:
                        pe.wait_ge(x_in[n], 16)
                    else:
                        pe.wait_ge(ln_x, (r - 1) * NT + n + 1)
                    for h in range(2):
                        if r > 0 and n == NT - 1 and h == 1:
                            pe.wait_ge(ln_last, r)
                        for k in range(4):
                            c = 4 * h + k
                            ins = pe.transpose(bank[2 * n + h][:, k * P:(k + 1) * P], x_tok[:, n, c * P:(c + 1) * P], ident[:])
                        ins.then_inc(xt_ps, 1)

            def first_slab(n, r, width, columns):
                hi, lo = columns(w_hi, n), columns(w_lo, n)
                pe.wait_ge(lo_done, n + 1)
                for t in range(2):
                    pe.wait_ge(xt_l, 8 * r + 4 * (t + 1))
                    tokens = slice(2 * t * P, 2 * (t + 1) * P)
                    for c in range(2):
                        if t == 0:
                            width(c)
                        for k in range(KT):
                            cols = (hi[:, c, k, :], lo[:, c, k, :]) if columns is w_pair else \
                                (hi[:, k, c * P:(c + 1) * P], lo[:, k, c * P:(c + 1) * P])
                            ins = three(bank[c][:, tokens], *cols, xt_hi[:, k, tokens], xt_lo[:, k, tokens],
                                        k == 0, k == KT - 1)
                        if t == 1:
                            ins.then_inc(half_slab, 1)

            def column_tile(n, c, psum):
                hi, lo = w_cols(w_hi, n), w_cols(w_lo, n)
                for k in range(KT):
                    ins = three(psum, hi[:, k, c * P:(c + 1) * P], lo[:, k, c * P:(c + 1) * P], xt_hi[:, k, :],
                                xt_lo[:, k, :], k == 0, k == KT - 1)
                ins.then_inc(half_slab, 1)

            def row_tiles(n, i, hi, lo, first, last, f0, turns=range(NT), by_token=False, closes=True, before=()):
                pe.wait_ge(lo_done, n + 1 + 2 * i)
                order = [(r, t) for t in turns for r in range(ROWS)] if last or by_token else \
                    [(r, t) for r in range(ROWS) for t in turns]
                for r, t in order:
                    if t == turns[0]:
                        pe.wait_ge(act_split, f0 + r + 1 + 2 * ROWS * i)
                    if r == 0:
                        for when, semaphore, value in before:
                            if when == t:
                                pe.wait_ge(semaphore, value)
                    wh, wl = w_rows(w_hi, n)[:, r, :], w_rows(w_lo, n)[:, r, :]
                    ah, al = hi[:, r, t * P:(t + 1) * P], lo[:, r, t * P:(t + 1) * P]
                    for q, (a, w) in enumerate(((ah, wh), (ah, wl), (al, wh))):
                        for h in range(2):
                            ins = pe.matmul(bank[2 * t + h][:], a, w[:, h * 512:(h + 1) * 512],
                                            start=first and r == 0 and q == 0, stop=last and r == ROWS - 1 and q == 2)
                    if closes and t == turns[-1]:
                        ins.then_inc(half_slab, 1)
                    elif last and r == ROWS - 1:
                        ins.then_inc(acc_tile, 1)

            def out_projection(base, hi, lo, f0, begun=False):
                for s in range(1 if begun else 0, KT // ROWS):
                    row_tiles(base + s, 0, hi, lo, s == 0, s == KT // ROWS - 1, f0 + ROWS * s)

            def attention(items, banks, tiles, s_s, s_read, per, bias, s_p, s_t, s_tout, s_v, s_yout, s_y, score, probs,
                          value, y, others=0, before_last=None):
                steps = attention_steps(items, C_GROUP if others == 0 else A_GROUP, others)
                for now in steps:
                    if now is steps[-1] and before_last is not None:
                        before_last()
                    for kind, i in now:
                        nb = tiles(i) if kind in "STV" else 4
                        if kind == "S":
                            if i >= 2:
                                pe.wait_ge(s_read, per * (i - 1))
                            for m in range(2):
                                q, k = score(i, m)
                                ins = pe.matmul(bank[(i % 2) * 2 + m][:, 0:nb * P], q, k, start=True, stop=bias is None)
                            if bias is not None:
                                for m in range(2):
                                    ins = pe.matmul(bank[(i % 2) * 2 + m][:, 0:nb * P], *bias(i), start=False, stop=True)
                            ins.then_inc(s_s, 1)
                        elif kind in "TYO":
                            use = banks[(kind, i)]
                            if kind != "O":
                                pe.wait_ge(s_p if kind == "T" else s_y, i + 1)
                            if use >= 2:
                                pe.wait_ge(s_tout, use - 1)
                            if kind == "T":
                                blocks = probs(i)
                            elif kind == "Y":
                                blocks = [y(i)[:, b * P:(b + 1) * P] for b in range(4)]
                            else:
                                src = (rw[:, RA], rw[:, RB], rw[:, RK], yt0[:, 4:8])[i // NT]
                                blocks = [src[:, j, (i % NT) * P:(i % NT + 1) * P] for j in range(B_TILES)]
                            for b, blk in enumerate(blocks):
                                ins = pe.transpose(bank[4 + use % 2][:, b * P:(b + 1) * P], blk, ident[:])
                            ins.then_inc(s_t, 1)
                        elif kind == "V":
                            pe.wait_ge(s_tout, banks[("T", i)] + 1)
                            if i == 0 and others:
                                pe.wait_ge(va_out, 1)
                            if i % 4 == 0 and i >= 8:
                                pe.wait_ge(s_yout, i // 4 - 1)
                            for dst, terms in value(i):
                                for b, (p, v) in enumerate(terms):
                                    ins = pe.matmul(bank[6 + i // 4 % 2][:, dst], p, v, start=b == 0, stop=b == len(terms) - 1)
                            ins.then_inc(s_v, 1)

            pe.wait_ge(consts_pool, 1)
            x_transposed(0)
            first_slab(0, 0, lambda c: pe.wait_ge(tile0_free, c + 1), w_cols)
            pe.wait_ge(par_rows, 16 * N_PARAM_DMAS)
            pe.transpose(bank[6][:, 0:N_CHAN + 1], prow[0:N_CHAN + 1, 0, :], ident[0:N_CHAN + 1, 0:N_CHAN + 1])
            for q in range(4):
                ins = pe.transpose(bank[7][:, q * CONV_HALF:(q + 1) * CONV_HALF], prow[0:CONV_HALF, 1 + q, :],
                                   ident[0:CONV_HALF, 0:CONV_HALF])
            ins.then_inc(par_ps, 1)

            def preparation(s):
                if s == 1:
                    pe.wait_ge(squashed, 3)
                    pe.wait_ge(consts_pool, 13)
                    for n in range(NT):
                        pe.matmul(bank[4 + n][:], ones_row[:], w0_row[:], start=True, stop=False)
                        pe.matmul(bank[4 + n][:], wa[0:HD, n * P:(n + 1) * P], w2a2[0:HD, :], start=False, stop=True) \
                            .then_inc(lora, 1)
                elif s == 2:
                    pe.wait_ge(lora_out, NT)
                    for j in range(B_TILES):
                        for n in range(NT):
                            ins = pe.matmul(bank[4 + j][:, n * P:(n + 1) * P], l_tok[:, n, j * P:(j + 1) * P], ucum[:],
                                            start=True, stop=True)
                        ins.then_inc(cums, 1)
                elif s == 3:
                    pe.wait_ge(kk_sq, B_TILES)
                    pe.wait_ge(centred, 3)
                    for j in range(B_TILES):
                        ins = pe.matmul(bank[4][0:HEADS, :], headsel[:, j, :], sq[:, j, :], start=j == 0,
                                        stop=j == B_TILES - 1)
                    ins.then_inc(kk_ss, 1)
                elif s == 4:
                    pe.wait_ge(kk_max, 1)
                    pe.wait_ge(centred, 3 * B_TILES)
                    for j in range(B_TILES):
                        pe.matmul(bank[4 + j][:], w2a2[HD:P, j * P:(j + 1) * P], wa[HD:P, :], start=True, stop=True) \
                            .then_inc(lora, 1)
                elif s == 5:
                    pe.wait_ge(kk_inv, 1)
                    for j in range(B_TILES):
                        pe.wait_ge(lora_out, NT + j + 1)
                        pe.matmul(bank[4 + j][:], headsel_t[:, j, :], rs, start=True, stop=True).then_inc(kk_bc, 1)
                elif s == 7:
                    pe.wait_ge(rk_done, B_TILES)
                    pe.wait_ge(rw_ready, 1)
                    for n in range(NT):
                        for j in range(B_TILES):
                            ins = pe.matmul(bank[4][:, n * HEADS + 2 * j:n * HEADS + 2 * j + 2],
                                            sq[:, j, n * P:(n + 1) * P], pairsel[:], start=True, stop=True)
                    ins.then_inc(bon_ps, 1)

            pe.wait_ge(lo_done, 2)
            for c in range(2):
                pe.wait_ge(tile0_free, 3 + c)
                column_tile(1, c, bank[2 + c])
            for s in range(2, W_OUT0):
                pe.wait_ge(lo_done, s + 1)
                for c in range(2):
                    t = 2 * s + c
                    pe.wait_ge(tile0_free, t + 1)
                    column_tile(s, c, bank[t % 4])
                    if c == 0:
                        preparation(s - 1)
            pe.wait_ge(tile0_free, 24)

            for n in range(NT):
                ins = pe.transpose(bank[6][:, n * P:(n + 1) * P], va_ch[:, n * P:(n + 1) * P], ident[:])
            ins.then_inc(va_ps, 1)
            pe.wait_ge(rw_ready, B_TILES + 1)

            def a_score(i, m):
                n, j = i // 4, i % 4
                lo = max(n - 1, 0) * P
                return (qa[m * HD:(m + 1) * HD, j, n * P:(n + 1) * P],
                        kdup[m * HD:(m + 1) * HD, j // 2, lo:(n + 1) * P])

            def a_probs(i):
                nb = 1 if i < 4 else 2
                return [sa[:, i % 3, m, (2 - nb + b) * P:(3 - nb + b) * P] for m in range(2) for b in range(nb)]

            def a_value(i):
                n, j = i // 4, i % 4
                nb = 1 if n == 0 else 2
                return [(slice((2 * j + m) * HD, (2 * j + m + 1) * HD),
                         [(pta[:, i % 2, (m * nb + b) * P:(m * nb + b + 1) * P],
                           va_tok[:, n + 1 - nb + b, (j // 2) * HD:(j // 2 + 1) * HD]) for b in range(nb)])
                        for m in range(2)]

            attention(A_ITEMS, A_BANKS, lambda i: 1 if i < 4 else 2, a_s, s_read=a_bias, per=2, bias=None, s_p=a_exp,
                      s_t=a_t, s_tout=a_tout, s_v=a_v, s_yout=a_y, s_y=a_y, score=a_score, probs=a_probs, value=a_value,
                      y=lambda g: ya[:, g % 2, :], others=TOK_GROUPS)

            def rw_step(n, step, h):
                q = bank[4 * h:4 * h + 4]
                c = slice(n * P, (n + 1) * P)
                if step in ("A0", "A1"):
                    if n > 0:
                        pe.wait_ge(rw_dve[h], nth(RW_DVE, n - 1, "Y"))
                    elif h == 1:
                        pe.wait_ge(a_tout, len(A_BANKS))
                    for hd in range(2) if step == "A0" else range(2, 4):
                        rows, j = slice(HD * (hd % 2), HD * (hd % 2) + HD), 2 * h + hd // 2
                        ar = rw[rows, RA:RR + 1, j, c]
                        pe.matmul(q[hd][:, 0:2 * P], rw[rows, RB, j, c], ar, start=True, stop=True)
                        ins = pe.matmul(q[hd][:, 2 * P:4 * P], rw[rows, RK, j, c], ar, start=True, stop=True)
                elif step == "AV":
                    pe.wait_ge(rw_dve[h], nth(RW_DVE, n, "A1"))
                    for hd in range(4):
                        col = (4 * h + hd) * HD
                        ins = pe.matmul(q[3][:, hd * HD:(hd + 1) * HD], mt[:, h, hd, 2, :], tok[:, V_TOK, n, col:col + HD],
                                        start=True, stop=True)
                elif step[0] == "T":
                    if step != "T0":
                        pe.wait_ge(rw_dve[h], nth(RW_DVE, n, "D" + step[1]))
                    for hd in range(4):
                        ins = pe.transpose(q[0][:, hd * P:(hd + 1) * P], tt[:, h, hd, :], ident[:])
                elif step[0] == "P":
                    pe.wait_ge(rw_act[h], nth(RW_ACT, n, "T" + str(int(step[1]) - 1)))
                    for hd in range(4):
                        ins = pe.matmul(q[1][:, hd * P:(hd + 1) * P], mt[:, h, hd, 0, :], tn[:, h, hd, :], start=True, stop=True)
                elif step[0] == "D":
                    pe.wait_ge(rw_act[h], nth(RW_ACT, n, "P" + step[1]))
                    for hd in range(4):
                        ins = pe.matmul(q[2][:, hd * P:(hd + 1) * P], pp[:, h, hd, :], tt[:, h, hd, :], start=True, stop=True)
                elif step == "HG":
                    pe.wait_ge(rw_dve[h], nth(RW_DVE, n, "D6"))
                    for hd in range(4):
                        ins = pe.matmul(q[0][:, hd * P:(hd + 1) * P], tt[:, h, hd, :], av_a[:, h, hd, :],
                                        start=True, stop=True)
                elif step == "R":
                    pe.wait_ge(rw_act[h], nth(RW_ACT, n, "HG"))
                    for hd in range(4):
                        rows, jj, col = slice(HD * (hd % 2), HD * (hd % 2) + HD), hd // 2, (4 * h + hd) * HD
                        g, hh = hg[:, h, hd, HD:P], hg[:, h, hd, 0:HD]
                        pe.matmul(q[1][rows, jj * P:(jj + 1) * P], g, mt[:, h, hd, 1, :], start=True, stop=True)
                        pe.matmul(q[1][rows, 2 * P + jj * HD:2 * P + (jj + 1) * HD], g, tok[:, B_TOK, n, col:col + HD],
                                  start=True, stop=True)
                        pe.matmul(q[3][rows, 2 * P + jj * HD:2 * P + (jj + 1) * HD], tok[:, B_TOK, n, col:col + HD], hh,
                                  start=True, stop=False)
                        ins = pe.matmul(q[3][rows, 2 * P + jj * HD:2 * P + (jj + 1) * HD], tok[:, K_TOK, n, col:col + HD],
                                        tok[:, V_TOK, n, col:col + HD], start=False, stop=True)
                else:
                    pe.wait_ge(rw_dve[h], nth(RW_DVE, n, "R"))
                    pe.wait_ge(rw_act[h], nth(RW_ACT, n, "R"))
                    if n > 0:
                        if h == 0:
                            pe.wait_ge(gn_out, n)
                        for jj in range(2 if n < NT - 1 else 0):
                            pe.matmul(q[3][:, jj * P:(jj + 1) * P], mbd[:, 2 * h + jj, :], zbd[:, 2 * h + jj, :],
                                      start=True, stop=True)
                    for jj in range(2):
                        if n > 0:
                            pe.matmul(q[2][:, jj * P:(jj + 1) * P], r2[:, h, jj, :], zbd[:, 2 * h + jj, :],
                                      start=True, stop=False, skip_group_check=True)
                        for e in range(2):
                            hd = 2 * jj + e
                            dst, col = q[2][:, hd * HD:(hd + 1) * HD], (4 * h + hd) * HD
                            pe.matmul(dst, mt[:, h, hd, 1, :], hg[:, h, hd, 0:HD], start=n == 0, stop=False,
                                      skip_group_check=True)
                            ins = pe.matmul(dst, mt[:, h, hd, 3, :], tok[:, V_TOK, n, col:col + HD], start=False,
                                            stop=True, skip_group_check=True)
                ins.then_inc(rw_pe[h], 1)

            def gn_transposes(n):
                pe.wait_ge(gn_pool, 3 * (n + 1))
                for j in range(B_TILES):
                    ins = pe.transpose(bank[GN_BANK[n]][:, j * P:(j + 1) * P], y_tok[:, j * P:(j + 1) * P], ident[:])
                ins.then_inc(gn_ps, 1)

            for n, step, h in recurrence_steps():
                rw_step(n, step, h)
                if step == "P6" and h == 0 and n > 0:
                    gn_transposes(n - 1)
            for h in range(2):
                pe.wait_ge(rw_dve[h], nth(RW_DVE, NT - 1, "Y"))
            def gate(j):
                pe.matmul(bank[4 + j][:], g2[:, j * P:(j + 1) * P], gate_in[:], start=True, stop=True).then_inc(gate_ps, 1)

            for j in range(B_TILES - 1):
                gate(j)
            row_tiles(W_OUT0, 0, yt_hi0, yt_lo0, True, False, 0, (0, 1), by_token=True, closes=False)
            gn_transposes(NT - 1)
            pe.wait_ge(gn_out, NT)
            gate(B_TILES - 1)
            pe.wait_ge(gated, B_TILES)
            row_tiles(W_OUT0, 0, yt_hi0, yt_lo0, True, False, 0, (2, 3), by_token=True)
            out_projection(W_OUT0, yt_hi0, yt_lo0, 0, begun=True)
            x_transposed(1)

            def mlp(base, layer, f0):
                first_slab(base, 2 * layer + 1, lambda u: pe.wait_ge(conv_d, layer * 5 * FT + 3 + u), w_pair)

                def up_tiles(s, i):
                    pe.wait_ge(lo_done, base + s + 1 + 2 * i)
                    hi, lo = w_pair(w_hi, base + s), w_pair(w_lo, base + s)
                    for u in range(2):
                        pe.wait_ge(conv_d, layer * 5 * FT + 5 * s + 3 + u + 10 * i)
                        for k in range(KT):
                            ins = three(bank[2 * s + u][:], hi[:, u, k, :], lo[:, u, k, :], xt_hi[:, k, :],
                                        xt_lo[:, k, :], k == 0, k == KT - 1)
                        ins.then_inc(half_slab, 1)

                up_tiles(1, 0)
                with pe.Fori(1, FT // 2) as i:
                    for s in range(2):
                        up_tiles(s, i)
                dn = base + FT
                row_tiles(dn, 0, act_hi, act_lo, True, False, f0, (2, 3, 0, 1), by_token=True,
                          before=((0, conv_d, 10 + (layer + 1) * 5 * FT),))
                with pe.Fori(0, (FT // ROWS - 3) // 2) as i:
                    for s in range(2):
                        row_tiles(dn + 1 + s, i, act_hi, act_lo, False, False, f0 + ROWS * (1 + s))
                for s in (FT // ROWS - 2, FT // ROWS - 1):
                    row_tiles(dn + s, 0, act_hi, act_lo, False, s == FT // ROWS - 1, f0 + ROWS * s)

            mlp(W_UP0, 0, KT)
            x_transposed(2)

            first_slab(W_IN1, 2, lambda c: pe.wait_ge(tile1_d, c + 1), w_cols)
            pe.wait_ge(lo_done, W_IN1 + 2)
            for c in range(2):
                pe.wait_ge(tile1_d, 3 + c)
                column_tile(W_IN1 + 1, c, bank[2 + c])
            for part in range(2):
                with pe.Fori(1 - part, 2) as i:
                    for s in range(2):
                        pe.wait_ge(lo_done, W_IN1 + 4 * part + s + 1 + 2 * i)
                        for c in range(2):
                            t = 2 * s + c
                            if part == 0:
                                pe.wait_ge(tile1_d, t + 1 + 4 * i)
                            elif t == 0:
                                pe.wait_ge(tile1_d, 12)
                                pe.wait_ge(tile1_a, t + 1 + 4 * i)
                            else:
                                pe.wait_ge(tile1_a, t + 1 + 4 * i)
                            column_tile(W_IN1 + s, c, bank[t][:])
            with pe.Fori(0, 2) as i:
                for s in range(2):
                    n = W_IN1 + 8 + s
                    pe.wait_ge(lo_done, n + 1 + 2 * i)
                    pe.wait_ge(tile1_d, 10 + 2 * s + 4 * i)
                    hi, lo = w_cols(w_hi, n), w_cols(w_lo, n)
                    for t in range(NT):
                        dst = bank[4 + 2 * s + t // 2][:, (t % 2) * COLS:(t % 2 + 1) * COLS]
                        for k in range(KT):
                            th, tl = xt_hi[:, k, t * P:(t + 1) * P], xt_lo[:, k, t * P:(t + 1) * P]
                            pe.matmul(dst, th, hi[:, k, :], start=k == 0, stop=False)
                            pe.matmul(dst, th, lo[:, k, :], start=False, stop=False)
                            ins = pe.matmul(dst, tl, hi[:, k, :], start=False, stop=k == KT - 1)
                        if t % 2:
                            ins.then_inc(half_slab, 1)
            pe.wait_ge(tile1_d, 20)
            pe.wait_ge(tile1_a, 12)
            pe.wait_ge(c_slopes, 1)

            def c_score(i, m):
                n, h = i // 8, i % 8
                return qc[m * HD:(m + 1) * HD, h, n * P:(n + 1) * P], kc[m * HD:(m + 1) * HD, h, 0:(n + 1) * P]

            def first_rows(turns, closes, before):
                row_tiles(W_OUT1, 0, yt_hi1, yt_lo1, True, False, KT + FT, turns, True, closes, before)

            attention(C_ITEMS, C_BANKS, lambda i: i // 8 + 1, c_s, s_read=c_exp, per=1,
                      bias=lambda i: (slope_id[:, i % 8, :], dist_c[:, (3 - i // 8) * P:4 * P]), s_p=c_p,
                      s_t=c_t, s_tout=c_tout, s_v=c_v, s_yout=c_yout, s_y=c_y, score=c_score,
                      probs=lambda i: [pc[:, i % 2, b * P:(b + 1) * P] for b in range(i // 8 + 1)],
                      value=lambda i: [(slice((i % 4) * P, (i % 4 + 1) * P),
                                        [(ptc[:, i % 2, b * P:(b + 1) * P], vc[:, b, (i % 8) * P:(i % 8 + 1) * P])
                                         for b in range(i // 8 + 1)])],
                      y=lambda g: yc[:, g % 2, :],
                      before_last=lambda: first_rows((0, 1, 3), False, ((3, c_yout, C_ITEMS // 4),)))
            first_rows((2,), True, ((2, c_tout, len(C_BANKS)),))
            out_projection(W_OUT1, yt_hi1, yt_lo1, KT + FT, begun=True)
            x_transposed(3)
            mlp(W_UP1, 1, 2 * KT + FT)

        @block.vector
        def _(dve):
            at = [0]

            def link(ins):
                at[0] += 1
                ins.then_inc(dve_at, 1)
                dve.wait_ge(dve_at, at[0])

            def x_low(r, n):
                for h in range(2):
                    dve.wait_ge(xt_h, 8 * r + 2 * n + h + 1)
                    view = (slice(None), slice(4 * h, 4 * h + 4), slice(n * P, (n + 1) * P))
                    dve.tensor_tensor(xt_lo[view], bank[2 * n + h].rearrange("p (k t) -> p k t", k=4),
                                      xt_hi[view].bitcast(F32), ALU.subtract).then_inc(xt_l, 1)

            def norm(l):
                gb = (ln_gb0, ln_gbf, ln_gb1, ln_gbf)[l]
                for stage, n in staggered((("statistics", 0), ("gain", 1), ("low", 3))):
                    if stage == "statistics":
                        if n < NT - 1:
                            dve.wait_ge(acc_tile, (NT - 1) * l + n + 1)
                        else:
                            dve.wait_ge(half_slab, 2 * (W_UP0, W_IN1, W_UP1, W_END)[l])
                        halves = [x_tok[:, n, h * 512:(h + 1) * 512] for h in range(2)]
                        for h, xs in enumerate(halves):
                            dve.scalar_tensor_tensor(out=xs, in0=xs, scalar=ALPHA, in1=bank[2 * n + h][:],
                                                     op0=ALU.mult, op1=ALU.add).then_inc(dve_at, 1)
                        for h, xs in enumerate(halves):
                            at[0] += 1
                            dve.wait_ge(dve_at, at[0])
                            ins = dve.bn_stats(bn2[:, n % 2, h, :], xs)
                            if h == 0:
                                ins.then_inc(dve_at, 1)
                        at[0] += 1
                        link(ins)
                        link(dve.bn_aggr(mv[:, n, :], bn2[:, n % 2]))
                        dve.tensor_scalar(neg_mean[:, n:n + 1], mv[:, n, 0:1], -1.0, None, ALU.mult).then_inc(ln_sum, 1)
                        dve.tensor_scalar(mv[:, n, 1:2], mv[:, n, 1:2], LN_EPS, None, ALU.add).then_inc(ln_sum, 1)
                    elif stage == "gain":
                        if n == 0:
                            dve.wait_ge(gb_in[l], 32)
                        for part, cols in enumerate(column_parts(n)):
                            done = l * (NT + 1) + n + part + 1
                            dve.wait_ge(ln_norm, done)
                            dve.tensor_tensor(x_tok[:, n, cols], x_tok[:, n, cols], gb[:, 0, cols], ALU.mult).then_inc(ln_mul, 1)
                            if part == 1:
                                dve.wait_ge(ln_mul, done)
                                dve.tensor_tensor(x_tok[:, n, cols], x_tok[:, n, cols], gb[:, 1, cols], ALU.add) \
                                    .then_inc(ln_last, 1)
                    elif l < 3:
                        x_low(l + 1, n)

            def row_tile(src, hi, lo, f, i, s, used):
                if used is not None:
                    dve.wait_ge(half_slab, used)
                dve.tensor_copy(hi[:, s, :], src).then_inc(act_split_h, 1)
                dve.wait_ge(act_split_h, f + 1 + 2 * i)
                dve.tensor_tensor(lo[:, s, :], src, hi[:, s, :].bitcast(F32), ALU.subtract).then_inc(act_split, 1)

            def attention(items, scores, s_s, s_max, s_exp, sink, finish_item, finish_group, others=0, before_mean=None):
                steps = attention_steps(items, C_GROUP if others == 0 else A_GROUP, others)
                for now in steps:
                    if now is steps[-3] and before_mean is not None:
                        before_mean()
                    for kind, i in now:
                        if kind == "S":
                            dve.wait_ge(s_s, i + 1)
                            if sink:
                                if i >= 3:
                                    dve.wait_ge(a_t, A_BANKS[("T", i - 3)] + 1)
                                for m in range(2):
                                    o, d, b = scores(i, m)
                                    dve.scalar_tensor_tensor(out=o, in0=d, scalar=-SLOPES[2 * (i % 4) + m], in1=b,
                                                             op0=ALU.mult, op1=ALU.add).then_inc(a_bias, 1)
                                dve.wait_ge(a_bias, 2 * i + 2)
                            both = scores(i, None)
                            if i > 0:
                                dve.wait_ge(s_max, i)
                            link(dve.tensor_reduce(maxes, both, AX_X, ALU.max))
                            if sink:
                                j = i % 4
                                link(dve.tensor_tensor(maxes, maxes, sinks[:, 2 * j:2 * j + 2], ALU.max))
                            ins = dve.tensor_scalar(neg_max[:, i % 2, :], maxes, -1.0, None, ALU.mult)
                            if sink:
                                link(ins)
                                ins = dve.tensor_tensor(sink_e[:, i % 2, :], sinks[:, 2 * j:2 * j + 2], neg_max[:, i % 2, :],
                                                        ALU.add)
                            ins.then_inc(s_max, 1)
                        elif kind == "C":
                            dve.wait_ge(s_exp, i + 1)
                            finish_item(i)
                        elif kind in "GHM":
                            finish_group(i, kind)

            dve.nop().then_inc(tile0_free, 4)
            dve.nop().then_inc(conv_d, 10)
            dve.nop().then_inc(tile1_d, 4)
            dve.wait_ge(consts_pool, 5)
            link(dve.tensor_copy(dist_f[:], iota_i[:, 0, :]))
            link(dve.scalar_tensor_tensor(out=dist_f[:], in0=dist_f[:], scalar=-1.0, in1=dist_f[:], op0=ALU.mult, op1=ALU.max))
            link(dve.tensor_copy(dist_a[:], dist_f[:, 2 * P:4 * P]))
            link(dve.memset(dist_f[0:HD, 4 * P - HD:4 * P], MASKED))
            link(dve.tensor_copy(dist_c[:], dist_f[:]))
            dve.memset(dist_a[0:HD, 0:HD], MASKED)
            dve.memset(dist_a[0:HD, 2 * P - HD:2 * P], MASKED)
            link(dve.memset(dist_a[HD:P, 0:P], MASKED))
            for n in range(NT):
                x_low(0, n)
            diff = iota_i[:, 1, 0:P]
            for q in range(4):
                link(dve.tensor_scalar(tri4[:, q, :], diff, 0.0, None, ALU.is_gt if q % 2 == 0 else ALU.is_ge))
            link(dve.tensor_scalar(ucum[:], diff, 0.0, DECAY_SCALE, ALU.is_ge, ALU.mult))
            link(dve.tensor_tensor(mask_t[:, 0, :], iota_i[:, 2, 0:P], iota_i[:, 3, 0:P], ALU.bitwise_xor))
            for k in range(LEVELS + 1):
                link(dve.tensor_scalar(mask_t[:, 1, :], mask_t[:, 0, :], k, None, ALU.logical_shift_right))
                link(dve.scalar_tensor_tensor(out=merge[:, k, :], in0=mask_t[:, 1, :], scalar=1.0, in1=tri4[:, 0, :],
                                              op0=ALU.is_equal, op1=ALU.mult))
            dve.wait_ge(par_ps, 1)
            link(dve.tensor_copy(chan[:], bank[6][:, 0:N_CHAN]))
            link(dve.tensor_scalar(one_minus[:], chan[:], -1.0, 1.0, ALU.mult, ALU.add))
            link(dve.tensor_scalar(sub_g[:], bank[6][:, N_CHAN:N_CHAN + 1], 1.0 - LAM_INIT, None, ALU.mult))
            dve.tensor_copy(conv[:].rearrange("p l c -> p (l c)"), bank[7][:, 0:DEPTH * N_CONV]).then_inc(consts_dve, 1)
            lam = lam_in[:].rearrange("p (a b) d -> p a b d", b=2)
            link(dve.tensor_tensor(lam_in[:, 0:4:2, :], lam[:, :, 0, :], lam[:, :, 1, :], ALU.mult))
            dve.tensor_reduce(lam_s[:, 0:2], lam_in[:, 0:4:2, :], AX_X, ALU.add).then_inc(consts_dve, 1)
            dve.wait_ge(squashed, 1)
            link(dve.memset(lam_c[:, 0:1], 1.0))
            dve.scalar_tensor_tensor(out=lam_c[:, 1:2], in0=lam_s[:, 3:4], scalar=-LAM_INIT, in1=lam_s[:, 2:3],
                                     op0=ALU.add, op1=ALU.subtract).then_inc(consts_dve, 1)

            def mix_target(t):
                if t == 0:
                    return wa[:]
                if t == 1:
                    return gate_in[:]
                j, which = (t - 2) % 4, (t - 2) // 4
                return (rw[:, RK, j, :], rw[:, RR, j, :], yt0[:, 4 + j, :])[which]

            def mix_row(t):
                return 12 + t if t < 2 else (4 + t - 2, t - 6, 8 + t - 10)[(t - 2) // 4]

            def mix(tiles):
                for t in tiles:
                    dve.wait_ge(mixed, t + 1)
                    o, r = mix_target(t), mix_row(t)
                    dve.scalar_tensor_tensor(out=o[:, 1:SEQ], in0=bank[t % 4][:, 0:SEQ - 1], scalar=chan[:, r:r + 1],
                                             in1=o[:, 1:SEQ], op0=ALU.mult, op1=ALU.add).then_inc(tile0_free, 1)

            def key_squares():
                for j in range(B_TILES):
                    dve.wait_ge(tile0_free, 4 + 2 + j + 1)
                    link(dve.tensor_scalar(rw[:, RA, j, :], rw[:, RK, j, :], chan[:, R_KK + j:R_KK + j + 1], None, ALU.mult))
                    dve.tensor_tensor(sq[:, j, :], rw[:, RA, j, :], rw[:, RA, j, :], ALU.mult).then_inc(kk_sq, 1)

            def centre_decays():
                for j in range(B_TILES):
                    dve.wait_ge(cums, j + 1)
                    ls = bank[4 + j][:].rearrange("p (n t) -> p n t", n=NT)
                    dve.tensor_scalar(cn[:, j, :], ls[:, :, P - 1], 0.5, None, ALU.mult).then_inc(centred, 1)
                    dve.wait_ge(centred, 3 * j + 1)
                    dve.tensor_scalar(epos[:, j, :, 0], cn[:, j, :], -1.0, None, ALU.mult).then_inc(centred, 1)
                    dve.tensor_tensor(epos[:, j, :, 1:P + 1], ls, cn[:, j, :].unsqueeze(2).to_broadcast([P, NT, P]),
                                      ALU.subtract).then_inc(centred, 1)
                dve.tensor_tensor(zsc, cn[:, :, 0:NT - 1], cn[:, :, 1:NT], ALU.add).then_inc(centred, 1)

            def scaled(j):
                c = lambda r: (chan[:, r + j:r + j + 1])
                A, K, KK, R = rw[:, RB, j, :], rw[:, RK, j, :], rw[:, RA, j, :], rw[:, RR, j, :]
                dve.wait_ge(key_factor, j + 1)
                link(dve.tensor_tensor(K, K, sq[:, j, :], ALU.mult))
                dve.scalar_tensor_tensor(out=sq[:, j, :], in0=R, scalar=c(R_RK), in1=K, op0=ALU.mult, op1=ALU.mult) \
                    .then_inc(rk_done, 1)
                dve.wait_ge(kk_bc, j + 1)
                link(dve.tensor_tensor(KK, KK, bank[4 + j][:], ALU.mult))
                link(dve.tensor_tensor(A, A, KK, ALU.mult))
                dve.wait_ge(exps, j + 1)
                v4 = lambda t: t.rearrange("p (n t) -> p n t", n=NT)
                dve.wait_ge(rk_done, j + 1)
                link(dve.tensor_tensor(v4(K), v4(K), eneg[:, j], ALU.mult))
                link(dve.tensor_tensor(v4(A), v4(A), eneg[:, j], ALU.mult))
                link(dve.tensor_tensor(v4(R), v4(R), epos[:, j, :, 1:P + 1], ALU.mult))
                dve.scalar_tensor_tensor(out=v4(KK), in0=v4(KK), scalar=-1.0, in1=epos[:, j, :, 0:P], op0=ALU.mult,
                                         op1=ALU.mult).then_inc(rw_ready, 1)

            mix(range(6))
            key_squares()
            mix(range(6, 8))
            centre_decays()
            mix(range(8, 10))
            dve.wait_ge(kk_ss, 1)
            dve.tensor_scalar(rs, bank[4][0:HEADS, :], 1e-24, None, ALU.max).then_inc(kk_max, 1)
            dve.wait_ge(kk_root, 1)
            dve.reciprocal(rs, rs).then_inc(kk_inv, 1)
            mix(range(10, 12))
            scaled(0)
            mix(range(12, 13))
            scaled(1)
            mix(range(13, 14))
            for j in range(2, B_TILES):
                scaled(j)
            dve.wait_ge(bon_ps, 1)
            dve.tensor_copy(bonus, bank[4][:, 0:NT * HEADS].rearrange("p (n h) -> p n h", n=NT)).then_inc(rw_ready, 1)
            dve.wait_ge(rw_ready, B_TILES + 1)
            for t in range(MIX_COUNT, MIX_COUNT + 4):
                dve.wait_ge(half_slab, t + 1)
                dve.tensor_scalar(qa[:, t - MIX_COUNT, :], bank[t % 4][:], HD ** -0.5, None, ALU.mult).then_inc(tile0_free, 1)
            dve.wait_ge(half_slab, 19)
            for kv in range(2):
                for e in range(2):
                    ins = dve.tensor_copy(kdup[e * HD:(e + 1) * HD, kv, :], bank[2][kv * HD:(kv + 1) * HD, :])
            ins.then_inc(tile0_free, 1)
            dve.wait_ge(half_slab, 20)
            dve.tensor_copy(va_ch[:], bank[3][:]).then_inc(tile0_free, 1)
            dve.wait_ge(va_ps, 1)
            dve.tensor_copy(va_tok[:].rearrange("p n c -> p (n c)"), bank[6][:]).then_inc(va_out, 1)

            def a_scores(i, m):
                w = P if i < 4 else 2 * P
                if m is None:
                    return sa[:, i % 3, :, 2 * P - w:2 * P]
                return sa[:, i % 3, m, 2 * P - w:2 * P], dist_a[:, 2 * P - w:2 * P], bank[(i % 2) * 2 + m][:, 0:w]

            def a_item(i):
                n, j = i // 4, i % 4
                link(dve.tensor_tensor(den[:, i % 2, :], den[:, i % 2, :], sink_e[:, i % 2, :], ALU.add))
                dve.reciprocal(rden[:, n % 2, 2 * j:2 * j + 2], den[:, i % 2, :]).then_inc(a_den, 1)

            def a_group(g, kind):
                dve.wait_ge(a_v, 4 * g + 4)
                dve.wait_ge(a_den, 4 * g + 4)
                if g >= 2:
                    dve.wait_ge(a_t, A_BANKS[("Y", g - 2)] + 1)
                dve.tensor_tensor(ya[:, g % 2, :].rearrange("p (h c) -> p h c", h=HEADS),
                                  bank[6 + g % 2][:].rearrange("p (h c) -> p h c", h=HEADS),
                                  rden[:, g % 2, :].unsqueeze(2).to_broadcast([P, HEADS, HD]), ALU.mult).then_inc(a_y, 1)

            attention(A_ITEMS, a_scores, a_s, a_max, a_exp, sink=True, finish_item=a_item, finish_group=a_group,
                      others=TOK_GROUPS)

            def rw_step(n, step, h):
                q = bank[4 * h:4 * h + 4]
                dve.wait_ge(rw_pe[h], nth(RW_PE, n, step))
                if step in ("A0", "A1"):
                    if n == 0:
                        dve.wait_ge(rw_init, h + 1)
                    for hd in range(2) if step == "A0" else range(2, 4):
                        ins = (dve.copy_predicated(mt[:, h, hd].rearrange("p m t -> p (m t)"),
                                                 tri4[:].rearrange("p m t -> p (m t)"), q[hd][:]))
                        if hd != 1:
                            link(ins)
                    if step == "A1":
                        dve.wait_ge(tt_ident[h], n + 1)
                        dve.wait_ge(rw_dve[h], nth(RW_DVE, n, "A0"))
                        ins = dve.copy_predicated(tt[:, h], merge[:, 0:1, :].to_broadcast([P, 4, P]), mt[:, h, :, 0, :])
                elif step[0] == "D":
                    k = int(step[1])
                    ins = dve.copy_predicated(tt[:, h], merge[:, k:k + 1, :].to_broadcast([P, 4, P]),
                                              q[2][:].rearrange("p (a t) -> p a t", a=4))
                elif step == "R":
                    dve.tensor_tensor(r2[:, h, 0:2], q[1][:, 0:2 * P].rearrange("p (a t) -> p a t", a=2),
                                      rw[:, RR, 2 * h:2 * h + 2, n * P:(n + 1) * P], ALU.add)
                    for e in range(2):
                        rows = slice(e * HD, (e + 1) * HD)
                        ins = dve.tensor_tensor(mbd[rows, 2 * h:2 * h + 2, rows],
                                                q[1][rows, 2 * P:3 * P].rearrange("p (a t) -> p a t", a=2),
                                                ident[rows, rows].unsqueeze(1).to_broadcast([HD, 2, HD]), ALU.add)
                else:
                    if n > 0 and h == 0:
                        dve.wait_ge(gn_ps, n)
                    dve.wait_ge(rw_act[h], nth(RW_ACT, n, "R"))
                    ins = dve.tensor_copy(y_tok[:, 4 * h * HD:4 * (h + 1) * HD], q[2][:, 0:2 * P])
                    if n < NT - 1:
                        nn = nst[:, 2 * h:2 * h + 2, :]
                        if n > 0:
                            for e in range(2):
                                rows = slice(e * HD, (e + 1) * HD)
                                link(dve.tensor_tensor(nn[rows], nn[rows],
                                                       q[3][:, 0:2 * P].rearrange("p (a c) -> p a c", a=2)[rows, :, rows],
                                                       ALU.add))
                        for e in range(2):
                            rows = slice(e * HD, (e + 1) * HD)
                            ins = dve.tensor_tensor(zbd[rows, 2 * h:2 * h + 2, rows], nn[rows],
                                                    zsc[rows, 2 * h:2 * h + 2, n:n + 1].to_broadcast([HD, 2, HD]), ALU.mult)
                ins.then_inc(rw_dve[h], 1)

            def group_norm(n, part):
                y8 = y_tok[:].rearrange("p (h c) -> p h c", h=HEADS)
                s8 = tok[:, A_TOK, n, :].rearrange("p (h c) -> p h c", h=HEADS)
                v8 = tok[:, V_TOK, n, :].rearrange("p (h c) -> p h c", h=HEADS)
                if part == 0:
                    for h in range(2):
                        dve.wait_ge(rw_dve[h], nth(RW_DVE, n, "Y"))
                    link(dve.tensor_reduce(gn_m, y8, AX_X, ALU.add))
                    link(dve.tensor_scalar(gn_m, gn_m, 1.0 / HD, None, ALU.mult))
                    dve.tensor_tensor(y8, y8, gn_m.unsqueeze(2).to_broadcast([P, HEADS, HD]), ALU.subtract) \
                        .then_inc(gn_dve, 1)
                elif part == 1:
                    dve.wait_ge(gn_pool, 3 * n + 1)
                    link(dve.tensor_reduce(gn_v, s8, AX_X, ALU.add))
                    dve.tensor_scalar(gn_v, gn_v, 1.0 / HD, GN_EPS, ALU.mult, ALU.add).then_inc(gn_dve, 1)
                elif part == 2:
                    dve.wait_ge(gn_pool, 3 * n + 2)
                    dve.tensor_tensor(y8, y8, gn_v.unsqueeze(2).to_broadcast([P, HEADS, HD]), ALU.mult).then_inc(gn_dve, 1)
                    dve.tensor_tensor(v8, v8, bonus[:, n, :].unsqueeze(2).to_broadcast([P, HEADS, HD]), ALU.mult) \
                        .then_inc(gn_dve, 1)

            dve.wait_ge(exps, B_TILES + 1)
            dve.wait_ge(consts_pool, 13)
            for n, step, h in recurrence_steps():
                if step in RW_DVE:
                    rw_step(n, step, h)
                for after, part in GN_AFTER:
                    if step == after and h == 1 and n > 0:
                        group_norm(n - 1, part)
            for part in range(3):
                group_norm(NT - 1, part)
                if part == 1:
                    for f in range(ROWS):
                        row_tile(yt0[:, f, :], yt_hi0, yt_lo0, f, 0, f, None)
            for j in range(B_TILES):
                dve.wait_ge(gate_ps, j + 1)
                dve.wait_ge(gn_out, NT)
                dve.tensor_tensor(yt0[:, 4 + j, :], yt0[:, 4 + j, :], bank[4 + j][:], ALU.mult).then_inc(gated, 1)

            def out_projection(base, yt, hi, lo, f0, begun=0):
                for f in range(begun, KT):
                    row_tile(yt[:, f, :], hi, lo, f0 + f, 0, f % 2, 2 * base + f - 1 if f >= 2 else None)

            def mlp(base, layer, f0):
                cw = conv[:, layer, :].rearrange("p (w u f) -> p w u f", w=4, u=2)
                def mix(s, i):
                    done = 10 + layer * 5 * FT + 5 * s
                    for w, back in ((1, 1), (0, 2)):
                        for u, buf in enumerate((cu, cg)):
                            if w == 1:
                                dve.wait_ge(conv_a, layer * 2 * FT + 2 * s + u + 1 + 4 * i)
                            else:
                                dve.wait_ge(conv_d, done + u + 1 + 10 * i)
                            dve.scalar_tensor_tensor(out=buf[:, s, back:SEQ], in0=bank[2 * s + u][:, 0:SEQ - back],
                                                     scalar=cw[:, w, u, bass.ds(2 * i + s, 1)], in1=buf[:, s, back:SEQ],
                                                     op0=ALU.mult, op1=ALU.add).then_inc(conv_d, 1)
                    dve.wait_ge(silu_a, layer * FT + s + 1 + 2 * i)
                    dve.tensor_tensor(act_t[:, bass.ds(2 * i + s, 1), :].rearrange("p o t -> p (o t)"), cu[:, s, :],
                                      cg[:, s, :], ALU.mult).then_inc(conv_d, 1)

                with dve.Fori(0, FT // 2 - 1) as i:
                    for s in range(2):
                        mix(s, i)
                for f in range(2):
                    dve.wait_ge(conv_d, 10 + layer * 5 * FT + 5 * (f + 1))
                    row_tile(act_t[:, f, :], act_hi, act_lo, f0 + f, 0, f, None)
                for s in range(2):
                    mix(s, FT // 2 - 1)
                dve.wait_ge(conv_d, 10 + (layer + 1) * 5 * FT)
                with dve.Fori(0, FT // 2 - 1) as i:
                    for s in range(2):
                        src = act_t[:, bass.ds(2 * i + 2 + s, 1), :].rearrange("p o t -> p (o t)")
                        row_tile(src, act_hi, act_lo, f0 + 2 + s, i, s, 2 * (base + FT) + s + 1 + 2 * i)

            dve.wait_ge(gated, B_TILES)
            out_projection(W_OUT0, yt0, yt_hi0, yt_lo0, 0, ROWS)
            norm(0)
            mlp(W_UP0, 0, KT)
            norm(1)

            with dve.Fori(0, 2) as i:
                for t in range(4):
                    dve.wait_ge(half_slab, 2 * W_IN1 + t + 1 + 4 * i)
                    dve.tensor_scalar(qc[:, bass.ds(4 * i + t, 1), :].rearrange("p o t -> p (o t)"), bank[t][:],
                                      HD ** -0.5, None, ALU.mult).then_inc(tile1_d, 1)
            with dve.Fori(0, 2) as i:
                for s in range(2):
                    for u in range(2):
                        dve.wait_ge(half_slab, 2 * W_IN1 + 16 + 2 * s + u + 1 + 4 * i)
                        dve.tensor_copy(vc[:, 2 * u:2 * u + 2, bass.ds(2 * COLS * i + COLS * s, COLS)],
                                        bank[4 + 2 * s + u][:].rearrange("p (n c) -> p n c", n=2)).then_inc(tile1_d, 1)

            for h in range(HEADS):
                ins = dve.tensor_scalar(slope_id[:, h, :], ident[:], -SLOPES[h], None, ALU.mult)
            ins.then_inc(c_slopes, 1)

            def c_scores(i, m):
                return bank_pair[i % 2][:, :, 0:P * (i // 8 + 1)]

            def c_item(i):
                w = P * (i // 8 + 1)
                link(dve.reciprocal(den[:, i % 2, :], den[:, i % 2, :]))
                link(dve.tensor_tensor(den[:, i % 2, :], den[:, i % 2, :], lam_c[:], ALU.mult))
                link(dve.tensor_scalar(sc[:, i % 2, 1, 0:w], sc[:, i % 2, 1, 0:w], den[:, i % 2, 1:2], None, ALU.mult))
                if i >= 2:
                    dve.wait_ge(c_t, C_BANKS[("T", i - 2)] + 1)
                dve.scalar_tensor_tensor(out=pc[:, i % 2, 0:w], in0=sc[:, i % 2, 0, 0:w], scalar=den[:, i % 2, 0:1],
                                         in1=sc[:, i % 2, 1, 0:w], op0=ALU.mult, op1=ALU.add).then_inc(c_p, 1)

            def c_group(g, kind):
                y4 = yc[:, g % 2, :].rearrange("p (h c) -> p h c", h=4)
                if kind == "H":
                    dve.wait_ge(c_square, g + 1)
                    dve.tensor_reduce(rms, ysq[:].rearrange("p (h c) -> p h c", h=4), AX_X, ALU.add).then_inc(c_sq, 1)
                    dve.wait_ge(c_sq, 2 * g + 1)
                    dve.tensor_scalar(rms, rms, 1.0 / P, SUBLN_EPS, ALU.mult, ALU.add).then_inc(c_sq, 1)
                elif kind == "M":
                    dve.wait_ge(c_rms, g + 1)
                    dve.tensor_tensor(y4, y4, rms.unsqueeze(2).to_broadcast([P, 4, P]), ALU.mult).then_inc(c_y, 1)

            def first_rows():
                dve.wait_ge(c_p, C_ITEMS)
                dve.wait_ge(c_tout, C_BANKS[("Y", C_ITEMS // 4 - 2)] + 1)
                for f in range(ROWS):
                    row_tile(yt1[:, f, :], yt_hi1, yt_lo1, KT + FT + f, 0, f, None)

            attention(C_ITEMS, c_scores, c_s, c_max, c_exp, sink=False, finish_item=c_item, finish_group=c_group,
                      before_mean=first_rows)
            dve.wait_ge(c_tout, len(C_BANKS))
            out_projection(W_OUT1, yt1, yt_hi1, yt_lo1, KT + FT, ROWS)
            norm(2)
            mlp(W_UP1, 1, 2 * KT + FT)
            norm(3)


N_PARAM_DMAS = 18

_INS = ['x', 'ln_g', 'ln_b', 'ev_w_in', 'ev_sinks', 'ev_mu', 'ev_w0', 'ev_w2', 'ev_a0', 'ev_a2', 'ev_g2', 'ev_k_k', 'ev_k_a',
        'ev_r_k', 'ev_gn_g', 'ev_gn_b', 'ev_w_out', 'od_w_in', 'od_lam', 'od_subln_g', 'od_w_out',
        'ffn_w_up', 'ffn_conv_w', 'ffn_conv_b', 'ffn_w_down']
_OUTS = [((1, SEQ, D), 'float32')]


def kernel(**inputs):
    import numpy as _np
    import concourse.bacc as _bacc
    from concourse import mybir as _mybir
    from concourse.bass_utils import run_bass_kernel_spmd as _run

    nc = _bacc.Bacc("TRN2", target_bir_lowering=False, num_devices=1)
    arrays, args = {}, []
    for name in _INS:
        a = _np.ascontiguousarray(inputs[name])
        arrays[f"in_{name}_dram"] = a
        args.append(nc.dram_tensor(f"in_{name}_dram", a.shape, _mybir.dt.from_np(a.dtype), kind="ExternalInput").ap())
    for i, (shape, dtype) in enumerate(_OUTS):
        dt = _mybir.dt.from_np(_np.dtype(dtype))
        args.append(nc.dram_tensor(f"out_{i}_dram", shape, dt, kind="ExternalOutput").ap())
    encoder(nc, *args)
    r = _run(nc, [arrays], core_ids=[0])
    return r.results[0]["out_0_dram"]
```
